# Optimizing a Trainium2 kernel written in Bass

```python
import jax
import jax.numpy as jnp
from jax import lax
import numpy as np

D_MODEL = 1024
BATCH = 1
SEQ = 1024
DEPTH = 1
DEC_BATCH = 8
DEC_SEQ = 8
PAST_LEN = 4096
PAGE_SIZE = 128

N_META = 16
MLA_HEADS = 8
MLA_Q_RANK = 256
MLA_KV_RANK = 128
MLA_NOPE = 64
MLA_ROPE = 32
MLA_V = 64
MLA_WIDTH = MLA_HEADS * MLA_V
MLA_SCALE = (MLA_NOPE + MLA_ROPE) ** -0.5
ROPE_THETA = 10000.0
Q_BLOCK = 128
HG_HEADS = 4
HG_DK = 128
HG_DV = 128
HG_WIDTH = HG_HEADS * HG_DV
HG_CHUNK = 64
N_EXPERTS = 64
TOP_K = 8
D_EXPERT = 256
D_SHARED = 256
ROUTED_SCALE = 2.5
MOE_BLOCK = 128
NORM_EPS = 1e-6
ALPHA = (2.0 * DEPTH) ** 0.25
BETA = (8.0 * DEPTH) ** -0.25
IN_SPLITS = (MLA_Q_RANK, MLA_KV_RANK, MLA_ROPE, HG_HEADS * HG_DK, HG_HEADS * HG_DK,
             HG_WIDTH, HG_WIDTH, D_MODEL, D_MODEL)
D_IN = MLA_Q_RANK + MLA_KV_RANK + MLA_ROPE + 2 * HG_HEADS * HG_DK + 2 * HG_WIDTH + 2 * D_MODEL

kernel_name = 'hybrid_mla_hgrn2_moe_step'

def rms_norm(x, g):
    xf = x.astype(jnp.float32)
    y = xf * lax.rsqrt(jnp.mean(xf * xf, axis=-1, keepdims=True) + NORM_EPS)
    return (y * g.astype(jnp.float32)).astype(x.dtype)

def layer_norm(x, g, b):
    xf = x.astype(jnp.float32)
    mu = jnp.mean(xf, axis=-1, keepdims=True)
    xc = xf - mu
    var = jnp.mean(xc * xc, axis=-1, keepdims=True)
    y = xc * lax.rsqrt(var + NORM_EPS)
    return (y * g.astype(jnp.float32) + b.astype(jnp.float32)).astype(x.dtype)

def rope_angles(pos):
    half = MLA_ROPE // 2
    inv = ROPE_THETA ** (-jnp.arange(half, dtype=jnp.float32) / half)
    ang = pos.astype(jnp.float32)[:, None] * inv[None, :]
    return jnp.cos(ang), jnp.sin(ang)

def apply_rope(x, cos, sin):
    half = MLA_ROPE // 2
    shape = (1, cos.shape[0]) + (1,) * (x.ndim - 3) + (half,)
    c = cos.reshape(shape).astype(x.dtype)
    s = sin.reshape(shape).astype(x.dtype)
    x1, x2 = x[..., :half], x[..., half:]
    return jnp.concatenate([x1 * c - x2 * s, x2 * c + x1 * s], axis=-1)

def mixer_inputs(x, cos, sin, lb, lp):
    B, T, _ = x.shape
    bounds = np.cumsum(np.array(IN_SPLITS))[:-1].tolist()
    cq_raw, ckv_raw, kr_raw, hq, hf, hi, hg_gate, gate_mla, gate_hg = jnp.split(x @ lp['w_in'], bounds, axis=-1)
    c_q = rms_norm(cq_raw, lp['q_norm'])
    q = (c_q @ lp['w_uq']).reshape(B, T, MLA_HEADS, MLA_NOPE + MLA_ROPE)
    q_rope = apply_rope(q[..., MLA_NOPE:], cos, sin)
    q_lat = jnp.einsum('bthn,chn->bthc', q[..., :MLA_NOPE], lp['w_uk'])
    c_kv = rms_norm(ckv_raw, lp['kv_norm'])
    k_rope = apply_rope(kr_raw, cos, sin)
    f = lb + (1.0 - lb) * jax.nn.sigmoid(hf.astype(jnp.float32))
    log_f = jnp.log(f)

    def heads(a):
        return a.reshape(B, T, HG_HEADS, -1).transpose(0, 2, 1, 3)

    hg = (heads(hq), heads((1.0 - f).astype(x.dtype)), heads(hi), heads(log_f))
    return (q_lat, q_rope, c_kv, k_rope), hg, (hg_gate, gate_mla, gate_hg)

def mla_prompt_attention(q_lat, q_rope, c_kv, k_rope):
    B, T = q_lat.shape[:2]
    nb = -(-T // Q_BLOCK)
    pad = nb * Q_BLOCK - T

    def padt(a):
        return jnp.pad(a, [(0, 0), (0, pad)] + [(0, 0)] * (a.ndim - 2))

    ql_p, qr_p, ckv_p, kr_p = padt(q_lat), padt(q_rope), padt(c_kv), padt(k_rope)
    k_idx = jnp.arange(nb * Q_BLOCK)

    def block(i):
        s0 = i * Q_BLOCK
        ql = lax.dynamic_slice_in_dim(ql_p, s0, Q_BLOCK, axis=1)
        qr = lax.dynamic_slice_in_dim(qr_p, s0, Q_BLOCK, axis=1)
        s = jnp.einsum('bqhc,bkc->bhqk', ql, ckv_p) + jnp.einsum('bqhr,bkr->bhqk', qr, kr_p)
        s = s.astype(jnp.float32) * MLA_SCALE
        q_idx = s0 + jnp.arange(Q_BLOCK)
        s = jnp.where(k_idx[None, :] <= q_idx[:, None], s, -jnp.inf)
        p = jax.nn.softmax(s, axis=-1).astype(ckv_p.dtype)
        return jnp.einsum('bhqk,bkc->bqhc', p, ckv_p)

    o = lax.map(block, jnp.arange(nb))
    o = jnp.moveaxis(o, 0, 1).reshape(B, nb * Q_BLOCK, MLA_HEADS, MLA_KV_RANK)
    return o[:, :T]

def mla_sample_attention(q_lat, q_rope, c_kv, k_rope, cache_ckv, cache_kr, page_table):
    DB, S = q_lat.shape[:2]
    c_past = cache_ckv[page_table].reshape(DB, -1, MLA_KV_RANK)
    kr_past = cache_kr[page_table].reshape(DB, -1, MLA_ROPE)
    past = c_past.shape[1]
    s_past = jnp.einsum('bqhc,bkc->bhqk', q_lat, c_past) + jnp.einsum('bqhr,bkr->bhqk', q_rope, kr_past)
    s_new = jnp.einsum('bqhc,bkc->bhqk', q_lat, c_kv) + jnp.einsum('bqhr,bkr->bhqk', q_rope, k_rope)
    causal = jnp.tril(jnp.ones((S, S), dtype=bool))
    s_new = jnp.where(causal, s_new.astype(jnp.float32), -jnp.inf)
    s = jnp.concatenate([s_past.astype(jnp.float32), s_new], axis=-1) * MLA_SCALE
    p = jax.nn.softmax(s, axis=-1).astype(c_kv.dtype)
    return (jnp.einsum('bhqk,bkc->bqhc', p[..., :past], c_past)
            + jnp.einsum('bhqk,bkc->bqhc', p[..., past:], c_kv))

def hgrn_chunk(S0, q, k, v, log_f):
    dt = q.dtype
    C = q.shape[2]
    cum = jnp.cumsum(log_f, axis=2)
    causal = jnp.tril(jnp.ones((C, C), dtype=bool))
    diff = cum[:, :, :, None, :] - cum[:, :, None, :, :]
    decay = jnp.exp(jnp.where(causal[None, None, :, :, None], diff, -jnp.inf)).astype(dt)
    attn = jnp.einsum('bhtd,bhsd,bhtsd->bhts', q, k, decay)
    o = (jnp.einsum('bhts,bhsv->bhtv', attn, v)
         + jnp.einsum('bhtd,bhdv->bhtv', q * jnp.exp(cum).astype(dt), S0))
    last = cum[:, :, -1:, :]
    S = (jnp.exp(last[:, :, 0, :]).astype(dt)[..., None] * S0
         + jnp.einsum('bhsd,bhsv->bhdv', k * jnp.exp(last - cum).astype(dt), v))
    return o, S.astype(S0.dtype)

def hgrn_prompt(q, k, v, log_f):
    B, H, T, _ = q.shape
    S0 = jnp.zeros((B, H, HG_DK, HG_DV), q.dtype)
    o_meta, S = hgrn_chunk(S0, q[:, :, :N_META], k[:, :, :N_META], v[:, :, :N_META], log_f[:, :, :N_META])
    L = T - N_META
    nc = L // HG_CHUNK

    def to_chunks(a):
        return jnp.moveaxis(a[:, :, N_META:].reshape(B, H, nc, HG_CHUNK, a.shape[-1]), 2, 0)

    def body(state, xs):
        o, state = hgrn_chunk(state, *xs)
        return state, o

    S, o_c = lax.scan(body, S, (to_chunks(q), to_chunks(k), to_chunks(v), to_chunks(log_f)))
    o_real = jnp.moveaxis(o_c, 0, 2).reshape(B, H, L, HG_DV)
    return jnp.concatenate([o_meta, o_real], axis=2), S

def swiglu(x, w_gate, w_up, w_down):
    return (jax.nn.silu(x @ w_gate) * (x @ w_up)) @ w_down

def moe(x, lp):
    N, D = x.shape
    scores = jax.nn.sigmoid((x @ lp['router_w']).astype(jnp.float32))
    _, idx = lax.top_k(scores + lp['router_bias'].astype(jnp.float32), TOP_K)
    gate = jnp.take_along_axis(scores, idx, axis=-1)
    gate = gate / jnp.sum(gate, axis=-1, keepdims=True) * ROUTED_SCALE
    A = N * TOP_K
    flat_e = idx.reshape(A)
    order = jnp.argsort(flat_e)
    sorted_e = flat_e[order]
    counts = jnp.bincount(flat_e, length=N_EXPERTS)
    starts = jnp.cumsum(counts) - counts
    padded = (counts + MOE_BLOCK - 1) // MOE_BLOCK * MOE_BLOCK
    pends = jnp.cumsum(padded)
    pstarts = pends - padded
    dest = pstarts[sorted_e] + (jnp.arange(A) - starts[sorted_e])
    n_blocks = -(-A // MOE_BLOCK) + N_EXPERTS
    R = n_blocks * MOE_BLOCK
    tok = order // TOP_K
    rows = jnp.zeros((R, D), x.dtype).at[dest].set(x[tok])
    block_e = jnp.minimum(jnp.searchsorted(pends, jnp.arange(n_blocks) * MOE_BLOCK, side='right'), N_EXPERTS - 1)
    w_g, w_u, w_d = lp['w_exp_gate'], lp['w_exp_up'], lp['w_exp_down']

    def expert_block(args):
        xb, e = args
        return swiglu(xb, w_g[e], w_u[e], w_d[e])

    y_rows = lax.map(expert_block, (rows.reshape(n_blocks, MOE_BLOCK, D), block_e)).reshape(R, D)
    y = y_rows[dest] * gate.reshape(A)[order][:, None].astype(x.dtype)
    routed = jax.ops.segment_sum(y, tok, num_segments=N)
    return routed + swiglu(x, lp['w_sh_gate'], lp['w_sh_up'], lp['w_sh_down'])

def layer_tail(x, o_lat, o_hg, gates, lp):
    B, T, _ = x.shape
    hg_gate, gate_mla, gate_hg = gates
    mla_o = jnp.einsum('bthc,chv->bthv', o_lat, lp['w_uv']).reshape(B, T, MLA_WIDTH)
    hg = o_hg.transpose(0, 2, 1, 3)
    hg = rms_norm(hg, lp['hg_norm']) * jax.nn.silu(hg_gate.reshape(B, T, HG_HEADS, HG_DV))
    hg = hg.reshape(B, T, HG_WIDTH)
    merged = (jax.nn.sigmoid(gate_mla) * (mla_o @ lp['w_br_mla'])
              + jax.nn.sigmoid(gate_hg) * (hg @ lp['w_br_hg']))
    x = layer_norm(ALPHA * x + merged @ lp['w_out'], lp['ln1_g'], lp['ln1_b'])
    ff = moe(x.reshape(B * T, D_MODEL), lp).reshape(B, T, D_MODEL)
    return layer_norm(ALPHA * x + ff, lp['ln2_g'], lp['ln2_b'])

def setup_inputs(seed: int = 0) -> dict:
    key = jax.random.key(seed)
    ks = jax.random.split(key, 32)
    f32 = jnp.float32

    def nrm(k, shape, scale):
        return jax.random.normal(k, shape, f32) * scale

    def gain(k, shape):
        return 1.0 + 0.02 * jax.random.normal(k, shape, f32)

    n_pages = PAST_LEN // PAGE_SIZE
    n_pool = (5 * DEC_BATCH * n_pages) // 4
    page_table = jax.random.permutation(ks[5], n_pool)[:DEC_BATCH * n_pages]
    page_table = page_table.reshape(DEC_BATCH, n_pages).astype(jnp.int32)
    return {
        'x_prompt': nrm(ks[0], (BATCH, SEQ, D_MODEL), 1.0),
        'x_sample': nrm(ks[1], (DEC_BATCH, DEC_SEQ, D_MODEL), 1.0),
        'cache_mla_ckv': nrm(ks[2], (DEPTH, n_pool, PAGE_SIZE, MLA_KV_RANK), 1.0),
        'cache_mla_krope': nrm(ks[3], (DEPTH, n_pool, PAGE_SIZE, MLA_ROPE), 1.0),
        'state_hgrn': nrm(ks[4], (DEPTH, DEC_BATCH, HG_HEADS, HG_DK, HG_DV), 0.5),
        'page_table': page_table,
        'meta_tokens': nrm(ks[6], (N_META, D_MODEL), 1.0),
        'hg_lb_logits': nrm(ks[7], (DEPTH + 1, HG_HEADS * HG_DK), 0.5),
        'w_in': nrm(ks[8], (DEPTH, D_MODEL, D_IN), D_MODEL ** -0.5),
        'q_norm': gain(ks[9], (DEPTH, MLA_Q_RANK)),
        'kv_norm': gain(ks[10], (DEPTH, MLA_KV_RANK)),
        'w_uq': nrm(ks[11], (DEPTH, MLA_Q_RANK, MLA_HEADS * (MLA_NOPE + MLA_ROPE)), MLA_Q_RANK ** -0.5),
        'w_uk': nrm(ks[12], (DEPTH, MLA_KV_RANK, MLA_HEADS, MLA_NOPE), MLA_KV_RANK ** -0.5),
        'w_uv': nrm(ks[13], (DEPTH, MLA_KV_RANK, MLA_HEADS, MLA_V), MLA_KV_RANK ** -0.5 * BETA),
        'hg_norm': gain(ks[14], (DEPTH, HG_DV)),
        'w_br_mla': nrm(ks[15], (DEPTH, MLA_WIDTH, D_MODEL), MLA_WIDTH ** -0.5 * BETA),
        'w_br_hg': nrm(ks[16], (DEPTH, HG_WIDTH, D_MODEL), HG_WIDTH ** -0.5 * BETA),
        'w_out': nrm(ks[17], (DEPTH, D_MODEL, D_MODEL), D_MODEL ** -0.5 * BETA),
        'ln1_g': gain(ks[18], (DEPTH, D_MODEL)),
        'ln1_b': nrm(ks[19], (DEPTH, D_MODEL), 0.02),
        'router_w': nrm(ks[20], (DEPTH, D_MODEL, N_EXPERTS), D_MODEL ** -0.5),
        'router_bias': nrm(ks[21], (DEPTH, N_EXPERTS), 0.01),
        'w_exp_gate': nrm(ks[22], (DEPTH, N_EXPERTS, D_MODEL, D_EXPERT), D_MODEL ** -0.5),
        'w_exp_up': nrm(ks[23], (DEPTH, N_EXPERTS, D_MODEL, D_EXPERT), D_MODEL ** -0.5),
        'w_exp_down': nrm(ks[24], (DEPTH, N_EXPERTS, D_EXPERT, D_MODEL), D_EXPERT ** -0.5 * BETA),
        'w_sh_gate': nrm(ks[25], (DEPTH, D_MODEL, D_SHARED), D_MODEL ** -0.5),
        'w_sh_up': nrm(ks[26], (DEPTH, D_MODEL, D_SHARED), D_MODEL ** -0.5),
        'w_sh_down': nrm(ks[27], (DEPTH, D_SHARED, D_MODEL), D_SHARED ** -0.5 * BETA),
        'ln2_g': gain(ks[28], (DEPTH, D_MODEL)),
        'ln2_b': nrm(ks[29], (DEPTH, D_MODEL), 0.02),
    }

def reference(x_prompt, x_sample, cache_mla_ckv, cache_mla_krope, state_hgrn, page_table,
              meta_tokens, hg_lb_logits, w_in, q_norm, kv_norm, w_uq, w_uk, w_uv, hg_norm,
              w_br_mla, w_br_hg, w_out, ln1_g, ln1_b, router_w, router_bias,
              w_exp_gate, w_exp_up, w_exp_down, w_sh_gate, w_sh_up, w_sh_down, ln2_g, ln2_b):
    B = x_prompt.shape[0]
    T = N_META + x_prompt.shape[1]
    meta = jnp.broadcast_to(meta_tokens.astype(x_prompt.dtype)[None], (B, N_META, D_MODEL))
    xp = jnp.concatenate([meta, x_prompt], axis=1)
    xs = x_sample
    cos_p, sin_p = rope_angles(jnp.arange(T))
    cos_s, sin_s = rope_angles(PAST_LEN + jnp.arange(x_sample.shape[1]))
    lb_all = jnp.cumsum(jax.nn.softmax(hg_lb_logits.astype(jnp.float32), axis=0), axis=0)

    ckv_p_l, kr_p_l, hg_p_l, ckv_s_l, kr_s_l, hg_s_l = [], [], [], [], [], []
    for l in range(DEPTH):
        lp = {
            'w_in': w_in[l], 'q_norm': q_norm[l], 'kv_norm': kv_norm[l], 'w_uq': w_uq[l],
            'w_uk': w_uk[l], 'w_uv': w_uv[l], 'hg_norm': hg_norm[l], 'w_br_mla': w_br_mla[l],
            'w_br_hg': w_br_hg[l], 'w_out': w_out[l], 'ln1_g': ln1_g[l], 'ln1_b': ln1_b[l],
            'router_w': router_w[l], 'router_bias': router_bias[l], 'w_exp_gate': w_exp_gate[l],
            'w_exp_up': w_exp_up[l], 'w_exp_down': w_exp_down[l], 'w_sh_gate': w_sh_gate[l],
            'w_sh_up': w_sh_up[l], 'w_sh_down': w_sh_down[l], 'ln2_g': ln2_g[l], 'ln2_b': ln2_b[l],
        }
        lb = lb_all[l]
        (ql, qr, ckv, kr), (hq, hk, hv, hlf), gates = mixer_inputs(xp, cos_p, sin_p, lb, lp)
        o_lat = mla_prompt_attention(ql, qr, ckv, kr)
        o_hg, S_p = hgrn_prompt(hq, hk, hv, hlf)
        ckv_p_l.append(ckv)
        kr_p_l.append(kr)
        hg_p_l.append(S_p)
        xp = layer_tail(xp, o_lat, o_hg, gates, lp)
        (ql, qr, ckv, kr), (hq, hk, hv, hlf), gates = mixer_inputs(xs, cos_s, sin_s, lb, lp)
        o_lat = mla_sample_attention(ql, qr, ckv, kr, cache_mla_ckv[l], cache_mla_krope[l], page_table)
        o_hg, S_s = hgrn_chunk(state_hgrn[l], hq, hk, hv, hlf)
        ckv_s_l.append(ckv)
        kr_s_l.append(kr)
        hg_s_l.append(S_s)
        xs = layer_tail(xs, o_lat, o_hg, gates, lp)

    y_prompt = xp[:, N_META:]
    y_sample = xs
    new_ckv_prompt = jnp.stack(ckv_p_l, axis=0)
    new_krope_prompt = jnp.stack(kr_p_l, axis=0)
    new_hgrn_prompt = jnp.stack(hg_p_l, axis=0)
    new_ckv_sample = jnp.stack(ckv_s_l, axis=0)
    new_krope_sample = jnp.stack(kr_s_l, axis=0)
    new_hgrn_sample = jnp.stack(hg_s_l, axis=0)
    return (y_prompt, y_sample, new_ckv_prompt, new_krope_prompt, new_hgrn_prompt,
            new_ckv_sample, new_krope_sample, new_hgrn_sample)


_drawn_inputs = setup_inputs


def setup_inputs(seed=0):
    import zlib

    import numpy as np

    out = dict(_drawn_inputs(seed))
    spreads = {}
    factors = {'cache_mla_ckv': 5.396,
     'cache_mla_krope': 5.469,
     'q_norm': 8.0,
     'hg_norm': 5.393,
     'ln2_g': 2.737,
     'ln2_b': 2.93}
    for name, (base, spread) in spreads.items():
        noise = np.random.default_rng([zlib.crc32(name.encode()), seed]).standard_normal(out[name].shape)
        drawn = base * np.exp(spread * noise) if base else spread * noise
        out[name] = jnp.asarray(drawn.astype(out[name].dtype))
    for name, factor in factors.items():
        out[name] = (out[name] * factor).astype(out[name].dtype)
    return out
```

```python
import concourse.bass as bass
from concourse import mybir
from contextlib import ExitStack
import numpy as np

F32 = mybir.dt.float32
F32R = mybir.dt.float32r
BF16 = mybir.dt.bfloat16
I32 = mybir.dt.int32
ALU = mybir.AluOpType
ACT = mybir.ActivationFunctionType
AX = mybir.AxisListType

DM, SEQ, N_META, SAMPLES, NEW, PAST, PAGE = 1024, 1024, 16, 8, 8, 4096, 128
HEADS, NOPE, ROPE, VDIM, QRANK, CKV = 8, 64, 32, 64, 256, 128
HGH, HGD = 4, 128
EXPERTS, TOPK, DEXP = 64, 8, 256
EPS = 1e-6
ALPHA = 2.0 ** 0.25
SCALE = (NOPE + ROPE) ** -0.5
ROUTED_SCALE = 2.5
NEG = -1e30

TP = N_META + SEQ
TS = SAMPLES * NEW
T = TP + TS
NT = -(-T // 128)
LAST = T - 128 * (NT - 1)
TAIL = TP - 128 * (NT - 1)
NCH = 3
CH = T // NCH
KD = DM // 128
C_Q, C_KV, C_KR = 0, QRANK, QRANK + CKV
C_HQ = C_KR + ROPE
C_HF = C_HQ + HGH * HGD
C_HI = C_HF + HGH * HGD
C_HG = C_HI + HGH * HGD
C_GA = C_HG + HGH * HGD
C_GB = C_GA + DM
D_IN = C_GB + DM
CAP = 192
HALF = CAP // 2
VCAP = -(-T // CAP) * CAP
KOVER = VCAP // CAP - 1
SLOTS = EXPERTS * VCAP + CAP
NBLK_MAX = EXPERTS + (T * TOPK) // CAP + 2


def rows(i):
    return 128 if i < NT - 1 else LAST


class Arena:

    def __init__(self, tensor, words):
        self.tensor, self.words, self.at = tensor, words, 0

    def take(self, *shape):
        n = int(np.prod(shape))
        v = self.tensor[:, self.at:self.at + n]
        self.at += n
        assert self.at <= self.words, (self.at, self.words)
        if len(shape) == 2:
            v = v.rearrange("p (a b) -> p a b", a=shape[0])
        if len(shape) == 3:
            v = v.rearrange("p (a b c) -> p a b c", a=shape[0], b=shape[1])
        if len(shape) == 4:
            v = v.rearrange("p (a b c d) -> p a b c d", a=shape[0], b=shape[1], c=shape[2])
        return v


class Steps:

    def __init__(self, eng, sem):
        self.eng, self.sem, self.n = eng, sem, 0

    def did(self, ins):
        ins.then_inc(self.sem, 1)
        self.n += 1
        return self.n

    def settle(self):
        self.eng.wait_ge(self.sem, self.n)

    def link(self, ins):
        self.did(ins)
        self.settle()


def stage_latents(nc, S, I, O):
    arena, PS = S.arena, S.psum
    mark = arena.at
    S.ones = arena.take(128)
    xrow = arena.take(3, DM)
    wcol = arena.take(2, KD, 128)
    wkr = arena.take(2, KD, ROPE)
    sq = arena.take(3, T)
    cosT, sinT = arena.take(T), arena.take(T)
    rstd = arena.take(T)
    cqT = arena.take(2, T)
    ra, rb = arena.take(T), arena.take(T)
    qn = arena.take(2, T)
    wnope, wrope, wswap = arena.take(2, HEADS * NOPE), arena.take(2, HEADS * ROPE), arena.take(2, HEADS * ROPE)
    wuk = arena.take(HEADS * NOPE)
    ukT = arena.take(4, 128)
    krrow = arena.take(NT, ROPE)
    gq, gkv = arena.take(2), arena.take(1)
    sem = S.sem
    x_in = [sem(f"x_in{i}") for i in range(3)]
    x_turned, xT_ready = sem("x_turned"), [sem("xT_act"), sem("xT_dve")]
    consts, w_small, ones_ready = sem("l_consts"), sem("l_wsmall"), sem("l_ones")
    w_in = [sem("l_w0"), sem("l_w1")]
    wkr_in = sem("l_wkr")
    group_full = sem("l_full")
    group_free = [sem("l_free0"), sem("l_free1")]
    c_ready, rooted = sem("l_c"), sem("l_rooted")
    ukT_full, ukT_ready = sem("l_ukf"), sem("l_uk")
    row_full, row_free, kv_out, dve_own = sem("l_rowf"), sem("l_rowe"), sem("l_out"), sem("l_dve")

    groups = [("cq", 0), ("cq", 1), ("ckv", 0), ("kr", 0), ("krs", 0), ("nq", 0), ("nkv", 0)]
    for p in range(4):
        groups += [("qn", p)]
        if p < 2:
            groups += [("rope", p), ("ropes", p)]
        groups += [("lat", 2 * p), ("lat", 2 * p + 1)]
    on_act = ("cq", "ckv", "qn", "lat")
    W_SMALL = 16 * (5 + 2 * 4)
    nq = groups.index(("nq", 0))
    row_banks = [(S.ckv_rows, CKV, 0, 4, 128), (S.ckv_rows, CKV, 4, 4, 128), (S.ckv_rows, CKV, 8, 1, LAST),
                 (krrow, ROPE, 0, 8, 128), (krrow, ROPE, 8, 1, LAST)]

    def evacuated(eng, g):
        eng.wait_ge(group_free[g % 2], g // 2 + 1)

    def bank3(g):
        return PS[:, 3 * (g % 2):3 * (g % 2) + NCH, 0:CH]

    def col3(v):
        return v.rearrange("p (n c) -> p n c", n=NCH)

    block = S.block()

    @block.sync
    def _(sp):
        sp.dma_start(S.ident, I["c_ident"]).then_inc(consts, 16)
        for i in range(NT):
            if i >= 3:
                sp.wait_ge(x_turned, 2 * (i - 2))
            s = xrow[:, i % 3]
            if i == 0:
                sp.dma_start(s[0:N_META], I["meta_tokens"]).then_inc(x_in[0], 16)
                sp.dma_start(s[N_META:128], I["x_prompt"][0, 0:128 - N_META]).then_inc(x_in[0], 16)
            elif i < NT - 1:
                sp.dma_start(s, I["x_prompt"][0, 128 * i - N_META:128 * (i + 1) - N_META]).then_inc(x_in[i % 3], 16)
            else:
                sp.dma_start(s[0:TAIL], I["x_prompt"][0, SEQ - TAIL:SEQ]).then_inc(x_in[i % 3], 16)
                sp.dma_start(s[TAIL:LAST], I["x_sample"].rearrange("s n d -> (s n) d")).then_inc(x_in[i % 3], 16)
        for g, c in enumerate((C_Q, C_Q + 128, C_KV)):
            if g >= 2:
                sp.wait_ge(group_full, g - 1)
            sp.dma_start(wcol[:, g % 2], I["w_in"][0, :, c:c + 128].rearrange("(k p) n -> p k n", p=128)).then_inc(w_in[g % 2], 16)
        sp.wait_ge(row_free, 5)
        v = lambda o: o.rearrange("a b t c -> (a b t) c")
        w = lambda o: o.rearrange("a s n c -> (a s n) c")
        full = 128 * (NT - 1)
        for dst, dsts, src in ((O[2], O[5], S.ckv_rows), (O[3], O[6], krrow)):
            sp.dma_start(v(dst)[0:full].rearrange("(i p) c -> p i c", p=128), src[:, 0:NT - 1]).then_inc(kv_out, 16)
            sp.dma_start(v(dst)[full:TP], src[0:TAIL, NT - 1]).then_inc(kv_out, 16)
            sp.dma_start(w(dsts), src[TAIL:LAST, NT - 1]).then_inc(kv_out, 16)
        sp.wait_ge(kv_out, 6 * 16)

    @block.gpsimd
    def _(pool):
        kr = I["w_in"][0, :, C_KR:C_KR + ROPE].rearrange("(k p) n -> p k n", p=128)
        h = ROPE // 2
        pool.dma_start(wkr[:, 0], kr).then_inc(wkr_in, 16)
        pool.dma_start(wkr[:, 1, :, 0:h], kr[:, :, h:ROPE]).then_inc(wkr_in, 16)
        pool.dma_start(wkr[:, 1, :, h:ROPE], kr[:, :, 0:h]).then_inc(wkr_in, 16)
        for dst, src in ((cosT, I["c_cos"]), (sinT, I["c_sin"]),
                         (gq, I["q_norm"][0].rearrange("(j p) -> p j", p=128)),
                         (gkv, I["kv_norm"].rearrange("a p -> p a")),
                         (wuk, I["w_uk"][0].rearrange("c h n -> c (h n)"))):
            pool.dma_start(dst, src, allow_slow_non_contiguous=True).then_inc(w_small, 16)
        for j in range(2):
            uq = I["w_uq"][0, 128 * j:128 * (j + 1)].rearrange("p (h n) -> p h n", h=HEADS)
            sw = wswap[:, j].rearrange("p (h n) -> p h n", h=HEADS)
            pool.dma_start(wnope[:, j].rearrange("p (h n) -> p h n", h=HEADS), uq[:, :, 0:NOPE]).then_inc(w_small, 16)
            pool.dma_start(wrope[:, j].rearrange("p (h n) -> p h n", h=HEADS), uq[:, :, NOPE:NOPE + ROPE]).then_inc(w_small, 16)
            pool.dma_start(sw[:, :, 0:h], uq[:, :, NOPE + h:NOPE + ROPE]).then_inc(w_small, 16)
            pool.dma_start(sw[:, :, h:ROPE], uq[:, :, NOPE:NOPE + h]).then_inc(w_small, 16)
        pool.memset(S.ones, 1.0).then_inc(ones_ready, 1)

    @block.tensor
    def _(pe):
        pe.wait_ge(consts, 16)
        for i in range(NT):
            pe.wait_ge(x_in[i % 3], {0: 32, 3: 48, 6: 64, 8: 64}.get(i, 16 * (i // 3 + 1)))
            for g in range(2):
                b = (2 * i + g) % 8
                if i >= 4:
                    pe.wait_ge(xT_ready[g], i - 3)
                for k in range(4):
                    ins = pe.transpose(PS[:, b, 128 * k:128 * k + rows(i)],
                                       xrow[0:rows(i), i % 3, 128 * (4 * g + k):128 * (4 * g + k + 1)],
                                       S.ident[0:rows(i), 0:rows(i)])
                ins.then_inc(x_turned, 1)
        pe.wait_ge(xT_ready[0], NT)
        pe.wait_ge(xT_ready[1], NT)

        def product(g, out, pairs):
            if g >= 2:
                pe.wait_ge(group_free[g % 2], g // 2)
            for n in range(NCH):
                for j, (w, x) in enumerate(pairs):
                    ins = pe.matmul(out[:, n], w, x[:, CH * n:CH * (n + 1)], start=(j == 0), stop=(j == len(pairs) - 1))
            ins.then_inc(group_full, 1)

        for g, (kind, a) in enumerate(groups):
            out = bank3(g)
            if kind in ("cq", "ckv"):
                pe.wait_ge(w_in[g % 2], 16 * (g // 2 + 1))
                product(g, out, [(wcol[:, g % 2, k], S.xT[:, k]) for k in range(KD)])
            elif kind in ("kr", "krs"):
                pe.wait_ge(wkr_in, 48)
                product(g, out[0:ROPE], [(wkr[:, int(kind == "krs"), k], S.xT[:, k]) for k in range(KD)])
            elif kind == "nq":
                evacuated(pe, 0)
                evacuated(pe, 1)
                pe.wait_ge(ones_ready, 1)
                product(g, out, [(S.ones, sq[:, j]) for j in range(2)])
            elif kind == "nkv":
                evacuated(pe, 2)
                product(g, out, [(S.ones, sq[:, 2])])
                pe.wait_ge(w_small, W_SMALL)
                for p in range(4):
                    ins = pe.transpose(PS[:, 6, 128 * p:128 * (p + 1)], wuk[:, 128 * p:128 * (p + 1)], S.ident)
                ins.then_inc(ukT_full, 1)
            elif kind == "qn":
                pe.wait_ge(c_ready, 2)
                product(g, out, [(wnope[:, j, 128 * a:128 * (a + 1)], cqT[:, j]) for j in range(2)])
            elif kind == "rope":
                product(g, out, [(wrope[:, j, 128 * a:128 * (a + 1)], cqT[:, j]) for j in range(2)])
            elif kind == "ropes":
                product(g, out, [(wswap[:, j, 128 * a:128 * (a + 1)], cqT[:, j]) for j in range(2)])
            elif kind == "lat":
                evacuated(pe, groups.index(("qn", a // 2)))
                pe.wait_ge(ukT_ready, 1)
                r = NOPE * (a % 2)
                product(g, out, [(ukT[r:r + NOPE, a // 2], qn[r:r + NOPE, (a // 2) % 2])])
        pe.wait_ge(c_ready, 3)
        for q, (dst, w, first, n, p) in enumerate(row_banks):
            if q == 0:
                pe.wait_ge(ukT_ready, 1)
            if q >= 2:
                pe.wait_ge(row_free, q - 1)
            src = S.ckvT if w == CKV else S.krT[0:ROPE]
            for i in range(first, first + n):
                ins = pe.transpose(PS[0:p, 6 + q % 2, w * (i - first):w * (i - first + 1)],
                                   src[:, 128 * i:128 * i + p], S.ident[0:w, 0:w])
            ins.then_inc(row_full, 1)

    def copy_xT(eng, i, g, copy):
        eng.wait_ge(x_turned, 2 * i + g + 1)
        src = PS[:, (2 * i + g) % 8].rearrange("p (k t) -> p k t", k=4)[:, :, 0:rows(i)]
        copy(S.xT[:, 4 * g:4 * g + 4, 128 * i:128 * i + rows(i)], src).then_inc(xT_ready[g], 1)

    @block.scalar
    def _(act):
        for i in range(NT):
            copy_xT(act, i, 0, act.copy)
        for g, (kind, a) in enumerate(groups):
            if kind not in on_act:
                continue
            act.wait_ge(group_full, g + 1)
            if kind == "cq":
                act.copy(col3(cqT[:, a]), bank3(g))
                act.activation(col3(sq[:, a]), bank3(g), ACT.Square).then_inc(group_free[g % 2], 1)
            elif kind == "ckv":
                act.copy(col3(S.ckvT), bank3(g))
                act.activation(col3(sq[:, 2]), bank3(g), ACT.Square).then_inc(group_free[g % 2], 1)
                for g in (nq, nq + 1):
                    evacuated(act, g)
                    act.activation(rstd, rstd, ACT.Sqrt).then_inc(rooted, 1)
            elif kind == "qn":
                if a >= 2:
                    act.wait_ge(group_full, groups.index(("lat", 2 * (a - 2) + 1)) + 1)
                act.copy(col3(qn[:, a % 2]), bank3(g)).then_inc(group_free[g % 2], 1)
            elif kind == "lat":
                act.mul(col3(S.qlat[:, a]), bank3(g), SCALE).then_inc(group_free[g % 2], 1)

    @block.vector
    def _(dve):
        own = Steps(dve, dve_own)
        for i in range(NT):
            copy_xT(dve, i, 1, dve.tensor_copy)
        dve.wait_ge(w_small, W_SMALL)

        def norm(g, n, dst, src, gain):
            if n == CKV:
                dve.wait_ge(c_ready, 2)
            dve.tensor_scalar(col3(rstd), bank3(g), 1.0 / n, EPS, ALU.mult, ALU.add).then_inc(group_free[g % 2], 1)
            dve.wait_ge(rooted, 1 + int(n == CKV))
            own.link(dve.reciprocal(rstd, rstd))
            for d, s, w in zip(dst, src, gain):
                dve.scalar_tensor_tensor(d, s, w, rstd, ALU.mult, ALU.mult).then_inc(c_ready, 1)

        for g, (kind, a) in enumerate(groups):
            if kind in on_act:
                continue
            dve.wait_ge(group_full, g + 1)
            if kind == "kr":
                dve.tensor_tensor(col3(ra)[0:ROPE], bank3(g)[0:ROPE], col3(cosT)[0:ROPE], ALU.mult).then_inc(group_free[g % 2], 1)
            elif kind == "krs":
                dve.tensor_tensor(col3(rb)[0:ROPE], bank3(g)[0:ROPE], col3(sinT)[0:ROPE], ALU.mult).then_inc(group_free[g % 2], 1)
                evacuated(dve, g - 1)
                evacuated(dve, g)
                own.link(dve.tensor_tensor(S.krT[0:ROPE], ra[0:ROPE], rb[0:ROPE], ALU.add))
            elif kind == "nq":
                norm(g, QRANK, [cqT[:, 0], cqT[:, 1]], [cqT[:, 0], cqT[:, 1]], [gq[:, 0:1], gq[:, 1:2]])
            elif kind == "nkv":
                norm(g, CKV, [S.ckvT], [S.ckvT], [gkv[:, 0:1]])
                dve.wait_ge(ukT_full, 1)
                dve.tensor_copy(ukT.rearrange("p a b -> p (a b)"), PS[:, 6]).then_inc(ukT_ready, 1)
            elif kind == "rope":
                dve.scalar_tensor_tensor(col3(ra), bank3(g), SCALE, col3(cosT), ALU.mult, ALU.mult).then_inc(group_free[g % 2], 1)
            elif kind == "ropes":
                dve.scalar_tensor_tensor(col3(rb), bank3(g), SCALE, col3(sinT), ALU.mult, ALU.mult).then_inc(group_free[g % 2], 1)
                evacuated(dve, g - 1)
                evacuated(dve, g)
                own.link(dve.tensor_tensor(S.qrope[:, a], ra, rb, ALU.add))
        for q, (dst, w, first, n, p) in enumerate(row_banks):
            dve.wait_ge(row_full, q + 1)
            dve.tensor_copy(dst[0:p, first:first + n],
                            PS[0:p, 6 + q % 2, 0:w * n].rearrange("p (i c) -> p i c", c=w)).then_inc(row_free, 1)

    S.close(block)
    arena.at = mark


def stage_prompt_attention(nc, S, I, O):
    arena, PS, sem = S.arena, S.psum, S.sem
    mark = arena.at
    QT = NT - 1
    krz = arena.take(4, T)
    ql, qr = arena.take(2, 128 * QT), arena.take(2, 128 * QT)
    probs = arena.take(2, 128 * QT)
    probsT = arena.take(QT, 128)
    oT = arena.take(128)
    mla_rows = arena.take(QT, HEADS * VDIM)
    sums, nmax, rinv = arena.take(4), arena.take(4), arena.take(4)
    causal = arena.take(128)
    causal_b = arena.take(64).bitcast(BF16)
    setup, wuv_in, krz_zero, krz_ready, bf_ready = sem("a_setup"), sem("a_wuv"), sem("a_krz0"), sem("a_krz"), sem("a_bf")
    q_staged, s_full, max_ready, p_ready = sem("a_q"), sem("a_s"), sem("a_max"), sem("a_p")
    lo_full, lo_copied, hi_full, hi_copied = sem("a_lof"), sem("a_loc"), sem("a_hif"), sem("a_hic")
    o_full, o_copied, r_full, r_ready, rinv_ready = sem("a_of"), sem("a_oc"), sem("a_rf"), sem("a_rr"), sem("a_ri")
    t_full, t_copied = sem("a_tf"), [sem("a_tc0"), sem("a_tc1")]
    UNITS = [(s, i) for s in range(2) for i in range(QT)]
    W = len(UNITS)
    HI = QT - 4

    def hi_count(it, w):
        return 2 * HI * it + sum(1 for x in range(w + 1) if UNITS[x][1] >= 4)

    block = S.block()

    @block.sync
    def _(sp):
        sp.dma_start(causal, I["c_causal"]).then_inc(setup, 16)
        sp.dma_start(S.wuv, I["w_uv"][0].rearrange("c h v -> c (h v)")).then_inc(wuv_in, 16)

    @block.gpsimd
    def _(pool):
        def stage_q(h, a, s):
            pool.tensor_copy(ql[:, s], h(S.qlat)).then_inc(q_staged, 1)
            pool.tensor_copy(qr[:, s], a(S.qrope)).then_inc(q_staged, 1)

        for s in range(2):
            stage_q(lambda v: v[:, s, 0:128 * QT], lambda v: v[:, 0, 0:128 * QT], s)
        with pool.Fori(0, HEADS // 2 - 1) as it:
            for s in range(2):
                pool.wait_ge(s_full, W * it + QT * (s + 1))
                stage_q(lambda v: v[:, bass.ds(2 * it + 2 + s, 1), 0:128 * QT].rearrange("p a t -> p (a t)"),
                        lambda v: v[:, bass.ds((it + 1) // 2, 1), 0:128 * QT].rearrange("p a t -> p (a t)"), s)

    @block.tensor
    def _(pe):
        pe.wait_ge(krz_ready, 4)
        pe.wait_ge(bf_ready, 2)
        pe.wait_ge(wuv_in, 16)
        with pe.Fori(0, HEADS // 2) as it:
            def scores(w):
                s, i = UNITS[w]
                if i == 0:
                    pe.wait_ge(q_staged, 4 * it + 2 * (s + 1))
                if w >= 2:
                    pe.wait_ge(p_ready, W * it + w - 1)
                keys = 128 * (i + 1)
                for c in range(-(-keys // 512)):
                    n = min(512, keys - 512 * c)
                    out = PS[:, 2 * (w % 2) + c, 0:n]
                    diag = i // 4 == c
                    pe.matmul(out, ql[:, s, 128 * i:128 * (i + 1)], S.ckvT[:, 512 * c:512 * c + n], start=True, stop=False)
                    ins = pe.matmul(out, qr[:, s, 128 * i:128 * (i + 1)],
                                    krz[:, bass.ds((it % 2) * 2 + s, 1), 512 * c:512 * c + n],
                                    start=False, stop=not diag)
                    if diag:
                        d = 128 * (i % 4)
                        ins = pe.matmul(PS[:, 2 * (w % 2) + c, d:d + 128], S.ident_b, causal_b, start=False, stop=True)
                ins.then_inc(s_full, 1)

            def turn(w):
                i = UNITS[w][1]
                pe.wait_ge(p_ready, W * it + w + 1)
                for j in range(i + 1):
                    if j == 4:
                        if hi_count(0, w) > 1:
                            pe.wait_ge(hi_copied, hi_count(it, w) - 1)
                    if j == 0 and w:
                        pe.wait_ge(lo_copied, W * it + w)
                    ins = pe.transpose(PS[:, 4 + j // 4, 128 * (j % 4):128 * (j % 4 + 1)],
                                       probs[:, w % 2, 128 * j:128 * (j + 1)], S.ident)
                    if j == min(3, i):
                        ins.then_inc(lo_full, 1)
                    elif j == i:
                        ins.then_inc(hi_full, 1)

            def values(w):
                i = UNITS[w][1]
                pe.wait_ge(lo_copied, W * it + w + 1)
                if i >= 4:
                    pe.wait_ge(hi_copied, hi_count(it, w))
                if w:
                    pe.wait_ge(o_copied, W * it + w)
                for j in range(i + 1):
                    ins = pe.matmul(PS[:, 6, 0:128], S.ckv_rows[:, j], probsT[:, j], start=(j == 0), stop=(j == i))
                ins.then_inc(o_full, 1)

            def out_rows(w):
                s, i = UNITS[w]
                pe.wait_ge(o_copied, W * it + w + 1)
                if w:
                    pe.wait_ge(r_ready, W * it + w)
                pe.matmul(PS[:, 7, 0:VDIM], oT, S.wuv[:, bass.ds((2 * it + s) * VDIM, VDIM)],
                          start=True, stop=True).then_inc(r_full, 1)

            for step in range(W + 3):
                if step < W:
                    scores(step)
                if step >= 3:
                    out_rows(step - 3)
                if 2 <= step < W + 2:
                    values(step - 2)
                if 1 <= step < W + 1:
                    turn(step - 1)
        pe.wait_ge(r_ready, W * (HEADS // 2))
        for i in range(QT):
            for k in range(4):
                ins = pe.transpose(PS[:, i, 128 * k:128 * (k + 1)], mla_rows[:, i, 128 * k:128 * (k + 1)], S.ident)
            ins.then_inc(t_full, 1)

    def copy_back(eng, g, copy):
        for i in range(g, QT, 2):
            eng.wait_ge(t_full, i + 1)
            copy(S.mlaT[:, :, 128 * i:128 * (i + 1)], PS[:, i].rearrange("p (k t) -> p k t", k=4)).then_inc(t_copied[g], 1)

    @block.scalar
    def _(act):
        act.wait_ge(krz_zero, 1)
        for j in range(4):
            act.copy(krz[ROPE * j:ROPE * (j + 1), j], S.krT[0:ROPE]).then_inc(krz_ready, 1)
        with act.Fori(0, HEADS // 2) as it:
            for step in range(W + 2):
                if step < W:
                    w = step
                    i = UNITS[w][1]
                    act.wait_ge(max_ready, W * it + w + 1)
                    if w >= 2:
                        act.wait_ge(lo_full, W * it + w - 1)
                        if UNITS[w - 2][1] >= 4:
                            act.wait_ge(hi_full, hi_count(it, w - 2))
                    if w >= 4:
                        act.wait_ge(rinv_ready, W * it + w - 3)
                    keys = 128 * (i + 1)
                    src = PS[:, 2 * (w % 2):2 * (w % 2) + 2].rearrange("p b c -> p (b c)")[:, 0:keys]
                    act.activation(probs[:, w % 2, 0:keys], src, ACT.Exp, bias=nmax[:, w % 4:w % 4 + 1],
                                   accum_out=sums[:, w % 4:w % 4 + 1]).then_inc(p_ready, 1)
                if step >= 2:
                    w = step - 2
                    act.wait_ge(o_full, W * it + w + 1)
                    act.copy(oT, PS[:, 6, 0:128]).then_inc(o_copied, 1)
                if 1 <= step < W + 1:
                    w = step - 1
                    n = min(4, UNITS[w][1] + 1)
                    act.wait_ge(lo_full, W * it + w + 1)
                    act.copy(probsT[:, 0:n].rearrange("p a b -> p (a b)"), PS[:, 4, 0:128 * n]).then_inc(lo_copied, 1)
        copy_back(act, 0, act.copy)

    @block.vector
    def _(dve):
        dve.memset(krz.rearrange("p a b -> p (a b)"), 0.0).then_inc(krz_zero, 1)
        dve.wait_ge(setup, 16)
        dve.tensor_copy(causal_b, causal).then_inc(bf_ready, 1)
        dve.tensor_copy(S.ident_b, S.ident).then_inc(bf_ready, 1)
        with dve.Fori(0, HEADS // 2) as it:
            for step in range(W + 3):
                if step < W:
                    w = step
                    keys = 128 * (UNITS[w][1] + 1)
                    dve.wait_ge(s_full, W * it + w + 1)
                    src = PS[:, 2 * (w % 2):2 * (w % 2) + 2].rearrange("p b c -> p (b c)")[:, 0:keys]
                    dve.tensor_reduce(nmax[:, w % 4:w % 4 + 1], src, AX.X, ALU.max, negate=True).then_inc(max_ready, 1)
                if step >= 3:
                    w = step - 3
                    s, i = UNITS[w]
                    dve.wait_ge(p_ready, W * it + w + 1)
                    dve.reciprocal(rinv[:, w % 4:w % 4 + 1], sums[:, w % 4:w % 4 + 1]).then_inc(rinv_ready, 1)
                    dve.wait_ge(rinv_ready, W * it + w + 1)
                    dve.wait_ge(r_full, W * it + w + 1)
                    dve.tensor_scalar(mla_rows[:, i, bass.ds((2 * it + s) * VDIM, VDIM)], PS[:, 7, 0:VDIM],
                                      rinv[:, w % 4:w % 4 + 1], None, ALU.mult).then_inc(r_ready, 1)
                if 1 <= step < W + 1 and UNITS[step - 1][1] >= 4:
                    w = step - 1
                    n = UNITS[w][1] + 1 - 4
                    dve.wait_ge(hi_full, hi_count(it, w))
                    dve.tensor_copy(probsT[:, 4:4 + n].rearrange("p a b -> p (a b)"), PS[:, 5, 0:128 * n]).then_inc(hi_copied, 1)
        copy_back(dve, 1, dve.tensor_copy)
        first = 128 * QT
        for p in range(4):
            for e in range(2):
                c = first + TAIL + NEW * (2 * p + e)
                dve.tensor_copy(S.qs_c[:, p, 64 * e:64 * (e + 1)].rearrange("p (h t) -> p h t", h=HEADS), S.qlat[:, :, c:c + NEW])
        dve.tensor_copy(S.qt_c.rearrange("p (h t) -> p h t", h=HEADS), S.qlat[:, :, first:first + TAIL])
        for h in range(HEADS):
            j = ROPE * (h % 4)
            src = S.qrope[j:j + ROPE, h // 4]
            dve.tensor_copy(S.qt_r[0:ROPE, TAIL * h:TAIL * (h + 1)], src[:, first:first + TAIL])
            for p in range(4):
                dst = S.qs_r[0:ROPE, p].rearrange("p (e h t) -> p e h t", e=2, h=HEADS)[:, :, h]
                dve.tensor_copy(dst, src[:, first + TAIL + 2 * NEW * p:first + TAIL + 2 * NEW * (p + 1)].rearrange("p (e t) -> p e t", e=2))

    S.close(block)
    arena.at = mark


def stage_sample_attention(nc, S, I, O):
    arena, PS, sem = S.arena, S.psum, S.sem
    mark = arena.at
    GROUPS = PAST // 512
    NG = GROUPS + 1
    RESTW = LAST
    TG = 3
    past_c = arena.take(2, 2 * GROUPS, 4 * CKV)
    past_r = arena.take(2, 2 * GROUPS, 4 * ROPE)
    sc = arena.take(2, PAST + RESTW)
    kT = arena.take(2, 2, 512)
    krT = arena.take(2, 2, 512)
    oX = arena.take(HEADS, LAST)
    smask_b = arena.take(4 * RESTW // 2).bitcast(BF16).rearrange("p (a b) -> p a b", a=4)
    tmask_b = arena.take(TAIL // 2).bitcast(BF16)
    gmax, esum = arena.take(2, NG), arena.take(2, NG)
    nmax, rinv = arena.take(2), arena.take(2)
    pages, eighth, index = (arena.take(2 * SAMPLES).bitcast(I32) for _ in range(3))
    smask, tmask = sc[:, 0, 0:4 * RESTW], sc[:, 0, 512:512 + TAIL]
    ql, qrl = S.qslot_c, S.qslot_r
    index_ready = sem("s_index")
    consts, pages_in, bf_ready = sem("s_consts"), sem("s_pages"), sem("s_bf")
    past_in = [[sem(f"s_past{a}{e}") for e in range(2)] for a in range(2)]
    q_staged = sem("s_q")
    kT_full, ck_copied, kr_copied = sem("s_ktf"), sem("s_ckc"), sem("s_krc")
    sc_full, sc_copied, g_maxed, maxed = sem("s_scf"), sem("s_scc"), sem("s_gmx"), sem("s_mx")
    p_ready, summed, scaled = sem("s_p"), sem("s_sum"), sem("s_scd")
    pt_full, pt_copied, o_full, o_moved = sem("s_ptf"), sem("s_ptc"), sem("s_of"), sem("s_om")
    rdone, m_full, m_done = sem("s_rinv"), sem("s_mf"), sem("s_md")

    def grp(it, s, g):
        return TG + 2 * NG * it + NG * s + g + 1

    def pair(it, s):
        return 1 + 2 * it + s + 1

    def width(g):
        return 512 if g < GROUPS else RESTW

    block = S.block()

    @block.sync
    def _(sp):
        sp.dma_start(pages, I["page_table"]).then_inc(pages_in, 16)
        sp.dma_start(eighth, I["c_eighth"]).then_inc(pages_in, 16)
        sp.dma_start(smask, I["c_smask"]).then_inc(consts, 16)
        sp.dma_start(tmask, I["c_tmask"]).then_inc(consts, 16)

    @block.gpsimd
    def _(pool):
        ckv = I["cache_mla_ckv"][0].rearrange("n (k r) c -> (n k) (r c)", r=16)
        kro = I["cache_mla_krope"][0].rearrange("n (k r) c -> (n k) (r c)", r=16)

        def load_pair(n):
            s = n % 2
            for hf in range(2):
                for e in range(2):
                    col = 2 * (2 * n + e) + hf
                    rows_of = bass.IndirectOffsetOnAxis(ap=index[:, col:col + 1], axis=0)
                    at = e * GROUPS + 4 * hf
                    pool.indirect_dma_start(out=past_c[:, s, at:at + 4].rearrange("p a c -> p (a c)"), out_offset=None,
                                            in_=ckv, in_offset=rows_of).then_inc(past_in[s][hf], 16)
                    pool.indirect_dma_start(out=past_r[:, s, at:at + 4].rearrange("p a c -> p (a c)"), out_offset=None,
                                            in_=kro, in_offset=rows_of).then_inc(past_in[s][hf], 16)

        def stage_q(n):
            pool.tensor_copy(ql[:, n % 2], S.qs_c[:, n]).then_inc(q_staged, 1)
            pool.tensor_copy(qrl[0:ROPE, n % 2], S.qs_r[0:ROPE, n]).then_inc(q_staged, 1)

        pool.wait_ge(index_ready, 1)
        for n in range(4):
            if n >= 2:
                pool.wait_ge(o_full, pair(0, n - 2))
            load_pair(n)
            stage_q(n)

    @block.tensor
    def _(pe):
        pe.wait_ge(bf_ready, 2)
        for g in range(TG):
            n = 512 if g < 2 else TAIL
            if g == 2:
                pe.wait_ge(sc_copied, 1)
            pe.matmul(PS[:, 4 + g % 2, 0:n], S.qt_c, S.ckvT[:, 512 * g:512 * g + n], start=True, stop=False)
            ins = pe.matmul(PS[:, 4 + g % 2, 0:n], S.qt_r[0:ROPE], S.krT[0:ROPE, 512 * g:512 * g + n], start=False, stop=g < 2)
            if g == 2:
                ins = pe.matmul(PS[:, 4, 0:n], S.ident_b, tmask_b, start=False, stop=True)
            ins.then_inc(sc_full, 1)

        def turn(s, g, done, n, before):
            pe.wait_ge(scaled, done)
            if before is not None:
                pe.wait_ge(pt_copied, before)
            for j in range(-(-n // 128)):
                k = min(128, n - 128 * j)
                ins = pe.transpose(PS[0:k, 6 + g % 2, 128 * j:128 * (j + 1)],
                                   sc[:, s, 512 * g + 128 * j:512 * g + 128 * j + k], S.ident)
            ins.then_inc(pt_full, 1)

        for g in range(TG):
            turn(0, g, g + 1, 512 if g < 2 else TAIL, g - 1 if g >= 2 else None)
        for g in range(TG):
            pe.wait_ge(pt_copied, g + 1)
            for j in range(4 if g < 2 else 1):
                k = 128 if g < 2 else TAIL
                buf = kT[:, g % 2, 0] if g < 2 else kT[:, 0, 1]
                ins = pe.matmul(PS[:, 0, 0:128], S.ckv_rows[0:k, 4 * g + j], buf[0:k, 128 * j:128 * (j + 1)],
                                start=(g == 0 and j == 0), stop=(g == 2))
        ins.then_inc(o_full, 1)

        with pe.Fori(0, 2) as it:
            def turn_keys(s, g, e):
                k = 2 * g + e
                if g % 4 == 0:
                    pe.wait_ge(past_in[s][g // 4], 64 * (it + 1))
                if k >= 2:
                    pe.wait_ge(ck_copied, 4 * GROUPS * it + 2 * GROUPS * s + k - 1)
                    pe.wait_ge(kr_copied, 4 * GROUPS * it + 2 * GROUPS * s + k - 1)
                elif s == 0:
                    pe.wait_ge(o_moved, pair(it, -1))
                for r in range(4):
                    pe.transpose(PS[:, e, 128 * r:128 * (r + 1)], past_c[:, s, e * GROUPS + g, CKV * r:CKV * (r + 1)], S.ident)
                for r in range(4):
                    ins = pe.transpose(PS[0:ROPE, 2 + e, 128 * r:128 * (r + 1)],
                                       past_r[:, s, e * GROUPS + g, ROPE * r:ROPE * (r + 1)], S.ident)
                ins.then_inc(kT_full, 1)

            def scores(s, g):
                if g == 0:
                    pe.wait_ge(q_staged, 4 * it + 2 * (s + 1))
                pe.wait_ge(sc_copied, grp(it, s, g) - 2)
                n = width(g)
                for e in range(2):
                    out = PS[64 * e:64 * (e + 1), 4 + g % 2, 0:n]
                    if g < GROUPS:
                        pe.wait_ge(ck_copied, 4 * GROUPS * it + 2 * GROUPS * s + 2 * g + e + 1)
                        pe.wait_ge(kr_copied, 4 * GROUPS * it + 2 * GROUPS * s + 2 * g + e + 1)
                    kc = kT[:, g % 2, e] if g < GROUPS else S.ckvT[:, T - RESTW:T]
                    kr = krT[0:ROPE, g % 2, e] if g < GROUPS else S.krT[0:ROPE, T - RESTW:T]
                    pe.matmul(out, ql[:, s, 64 * e:64 * (e + 1)], kc, start=True, stop=False, skip_group_check=True)
                    ins = pe.matmul(out, qrl[0:ROPE, s, 64 * e:64 * (e + 1)], kr, start=False, stop=True, skip_group_check=True)
                if g == GROUPS:
                    ins = pe.matmul(PS[:, 4 + g % 2, 0:n], S.ident_b, smask_b[:, bass.ds(2 * it + s, 1)].rearrange("p a b -> p (a b)"),
                                    start=False, stop=True, skip_group_check=True)
                ins.then_inc(sc_full, 1)

            def values(s, g):
                pe.wait_ge(pt_copied, grp(it, s, g))
                if g < GROUPS:
                    for j in range(4):
                        for e in range(2):
                            pe.matmul(PS[:, s, 64 * e:64 * (e + 1)], past_c[:, s, e * GROUPS + g, CKV * j:CKV * (j + 1)],
                                      kT[:, g % 2, 0, 128 * j + 64 * e:128 * j + 64 * (e + 1)],
                                      start=(g == 0 and j == 0 and e == 0), stop=False, skip_group_check=True)
                else:
                    pe.matmul(PS[:, s, 0:128], S.ckv_rows[0:RESTW, NT - 1], kT[0:RESTW, g % 2, 0, 0:128],
                              start=False, stop=True, skip_group_check=True).then_inc(o_full, 1)

            for s in range(2):
                for g in range(GROUPS + 2):
                    if g < GROUPS:
                        turn_keys(s, g, 0)
                        turn_keys(s, g, 1)
                    if g >= 1:
                        scores(s, g - 1)
            for s in range(2):
                for g in range(NG + 1):
                    if g < NG:
                        turn(s, g, grp(it, s, g), width(g), grp(it, s, g) - 2)
                    if g >= 1:
                        values(s, g - 1)
        pe.wait_ge(o_moved, 5)
        for h in range(HEADS):
            ins = pe.matmul(PS[VDIM * (h % 2):VDIM * (h % 2 + 1), 4, LAST * (h // 2):LAST * (h // 2 + 1)],
                            S.wuv[:, VDIM * h:VDIM * (h + 1)], oX[:, h], start=True, stop=True)
        ins.then_inc(m_full, 1)

    @block.scalar
    def _(act):
        def copy_scores(s, g, done, n):
            act.wait_ge(sc_full, done)
            act.copy(sc[:, s, 512 * g:512 * g + n], PS[:, 4 + g % 2, 0:n]).then_inc(sc_copied, 1)

        def exps(s, g, of, n):
            act.wait_ge(maxed, of)
            act.activation(sc[:, s, 512 * g:512 * g + n], sc[:, s, 512 * g:512 * g + n], ACT.Exp,
                           bias=nmax[:, s:s + 1], accum_out=esum[:, s, g:g + 1]).then_inc(p_ready, 1)

        def copy_turned(buf, g, done, n):
            act.wait_ge(pt_full, done)
            k = min(n, 128)
            w = 128 * -(-n // 128)
            act.copy(buf[0:k, 0:w], PS[0:k, 6 + g % 2, 0:w]).then_inc(pt_copied, 1)

        act.wait_ge(bf_ready, 2)
        for g in range(TG):
            copy_scores(0, g, g + 1, 512 if g < 2 else TAIL)
        for g in range(TG):
            exps(0, g, 1, 512 if g < 2 else TAIL)
        for g in range(TG):
            copy_turned(kT[:, g % 2, 0] if g < 2 else kT[:, 0, 1], g, g + 1, 512 if g < 2 else TAIL)

        with act.Fori(0, 2) as it:
            for s in range(2):
                for g in range(NG):
                    if g < GROUPS:
                        for e in range(2):
                            act.wait_ge(kT_full, 4 * GROUPS * it + 2 * GROUPS * s + 2 * g + e + 1)
                            if g >= 2:
                                act.wait_ge(sc_full, grp(it, s, g - 2))
                            act.copy(kT[:, g % 2, e], PS[:, e]).then_inc(ck_copied, 1)
                    if g >= 1:
                        if s == 0 and g == 1:
                            act.wait_ge(pt_full, TG + 2 * NG * it)
                        copy_scores(s, g - 1, grp(it, s, g - 1), width(g - 1))
                        if s == 1:
                            exps(0, g - 1, pair(it, 0), width(g - 1))
                copy_scores(s, NG - 1, grp(it, s, NG - 1), width(NG - 1))
                if s == 1:
                    exps(0, NG - 1, pair(it, 0), width(NG - 1))
            for s in range(2):
                for g in range(NG):
                    if s == 0:
                        exps(1, g, pair(it, 1), width(g))
                    if g >= 2:
                        pass
                    copy_turned(kT[:, g % 2, 0], g, grp(it, s, g), width(g))

    @block.vector
    def _(dve):
        dve.wait_ge(pages_in, 32)
        dve.scalar_tensor_tensor(index, pages, 8.0, eighth, ALU.mult, ALU.add).then_inc(index_ready, 1)
        dve.wait_ge(consts, 32)
        dve.tensor_copy(smask_b.rearrange("p a b -> p (a b)"), smask).then_inc(bf_ready, 1)
        dve.tensor_copy(tmask_b, tmask).then_inc(bf_ready, 1)
        ts = Steps(dve, rdone)

        def group_max(s, g, done, n):
            dve.wait_ge(sc_copied, done)
            dve.tensor_reduce(gmax[:, s, g:g + 1], sc[:, s, 512 * g:512 * g + n], AX.X, ALU.max).then_inc(g_maxed, 1)

        def whole_max(s, done, n):
            dve.wait_ge(g_maxed, done)
            dve.tensor_reduce(nmax[:, s:s + 1], gmax[:, s, 0:n], AX.X, ALU.max, negate=True).then_inc(maxed, 1)

        def inverse(s, done, of, n):
            dve.wait_ge(p_ready, done)
            dve.tensor_reduce(rinv[:, s:s + 1], esum[:, s, 0:n], AX.X, ALU.add).then_inc(summed, 1)
            dve.wait_ge(summed, of)
            dve.reciprocal(rinv[:, s:s + 1], rinv[:, s:s + 1]).then_inc(rdone, 1)
            dve.wait_ge(rdone, of)

        def scale(s, g, n):
            dve.tensor_scalar(sc[:, s, 512 * g:512 * g + n], sc[:, s, 512 * g:512 * g + n], rinv[:, s:s + 1], None,
                              ALU.mult).then_inc(scaled, 1)

        for g in range(TG):
            group_max(0, g, g + 1, 512 if g < 2 else TAIL)
        whole_max(0, TG, TG)
        inverse(0, TG, 1, TG)
        for g in range(TG):
            scale(0, g, 512 if g < 2 else TAIL)
        dve.wait_ge(o_full, 1)
        dve.tensor_copy(oX[:, :, 0:TAIL], PS[:, 0, 0:128].rearrange("p (h t) -> p h t", h=HEADS)).then_inc(o_moved, 1)
        with dve.Fori(0, 2) as it:
            for s in range(2):
                for g in range(NG):
                    if g < GROUPS:
                        for e in range(2):
                            dve.wait_ge(kT_full, 4 * GROUPS * it + 2 * GROUPS * s + 2 * g + e + 1)
                            if g >= 2:
                                dve.wait_ge(sc_full, grp(it, s, g - 2))
                            dve.tensor_copy(krT[0:ROPE, g % 2, e], PS[0:ROPE, 2 + e]).then_inc(kr_copied, 1)
                    if g >= 1:
                        group_max(s, g - 1, grp(it, s, g - 1), width(g - 1))
                group_max(s, NG - 1, grp(it, s, NG - 1), width(NG - 1))
                whole_max(s, grp(it, s, NG - 1), NG)
            for s in range(2):
                inverse(s, grp(it, s, NG - 1), pair(it, s), NG)
                for g in range(NG):
                    scale(s, g, width(g))
                dve.wait_ge(o_full, pair(it, s))
                for e in range(2):
                    ins = dve.tensor_copy(oX[:, :, bass.ds(TAIL + 2 * NEW * (2 * it + s) + NEW * e, NEW)],
                                          PS[:, s, 64 * e:64 * (e + 1)].rearrange("p (h t) -> p h t", h=HEADS))
                ins.then_inc(o_moved, 1)
        dve.wait_ge(m_full, 1)
        dve.tensor_copy(S.mlaT[:, :, 128 * (NT - 1):T], PS[:, 4, 0:4 * LAST].rearrange("p (a t) -> p a t", a=4)).then_inc(m_done, 1)

    S.close(block)
    arena.at = mark


def stage_recurrence_inputs(nc, S, I, O):
    arena, PS, sem = S.arena, S.psum, S.sem
    mark = arena.at
    wcol = arena.take(2, KD, 128)
    wrow = arena.take(KD, 1024)
    sig = arena.take(2, 512)
    logits, lb = arena.take(2, HGH), arena.take(3, HGH)
    w_in, wrow_in, small_in = [sem("h_w0"), sem("h_w1")], sem("h_wr"), sem("h_small")
    group_full, group_free, lb_ready, exp_ready, own_s = sem("h_full"), [sem("h_free0"), sem("h_free1")], sem("h_lb"), sem("h_exp"), sem("h_own")
    row_full, row_free, sig_ready = sem("h_rf"), [sem("h_re0"), sem("h_re1")], sem("h_sig")

    def bank3(g):
        return PS[:, 3 * (g % 2):3 * (g % 2) + NCH, 0:CH]

    def col3(v):
        return v.rearrange("p (n c) -> p n c", n=NCH)

    block = S.block()

    @block.sync
    def _(sp):
        sp.dma_start(logits, I["hg_lb_logits"].rearrange("a (j p) -> p a j", p=128), allow_slow_non_contiguous=True).then_inc(small_in, 16)
        sp.dma_start(S.gain_b, I["hg_norm"]).then_inc(small_in, 16)
        for g in range(2 * HGH):
            if g >= 2:
                sp.wait_ge(group_full, g - 1)
            c = (C_HF if g % 2 else C_HQ) + 128 * (g // 2)
            sp.dma_start(wcol[:, g % 2], I["w_in"][0, :, c:c + 128].rearrange("(k p) n -> p k n", p=128)).then_inc(w_in[g % 2], 16)
            if g == 1:
                sp.dma_start(wrow, I["w_in"][0, :, C_HI:C_HI + 1024].rearrange("(k p) n -> p k n", p=128)).then_inc(wrow_in, 16)

    @block.tensor
    def _(pe):
        for g in range(2 * HGH):
            pe.wait_ge(w_in[g % 2], 16 * (g // 2 + 1))
            if g >= 2:
                pe.wait_ge(group_free[g % 2], g // 2)
            for n in range(NCH):
                for k in range(KD):
                    ins = pe.matmul(bank3(g)[:, n], wcol[:, g % 2, k], S.xT[:, k, CH * n:CH * (n + 1)], start=(k == 0), stop=(k == KD - 1))
            ins.then_inc(group_full, 1)
        pe.wait_ge(wrow_in, 16)
        for i in range(NT):
            for g in range(2):
                if i == 0:
                    pe.wait_ge(group_free[g], HGH)
                elif i >= 2:
                    pe.wait_ge(row_free[g], i - 1)
                b = 2 * (i % 2) + g
                for k in range(KD):
                    ins = pe.matmul(PS[0:rows(i), b], S.xT[:, k, 128 * i:128 * i + rows(i)], wrow[:, k, 512 * g:512 * (g + 1)],
                                    start=(k == 0), stop=(k == KD - 1))
                ins.then_inc(row_full, 1)

    @block.scalar
    def _(act):
        for l in range(2):
            act.wait_ge(own_s, 3)
            ins = act.activation(logits[:, l], logits[:, l], ACT.Exp)
        ins.then_inc(exp_ready, 1)
        for g in range(2 * HGH):
            act.wait_ge(group_full, g + 1)
            if g % 2:
                act.activation(col3(S.hf[:, g // 2]), bank3(g), ACT.Sigmoid).then_inc(group_free[1], 1)
            else:
                act.copy(col3(S.hq[:, g // 2]), bank3(g)).then_inc(group_free[0], 1)
        for i in range(NT):
            r = rows(i)
            act.wait_ge(row_full, 2 * i + 1)
            act.copy(S.hrows[0:r, i, 0:512], PS[0:r, 2 * (i % 2)]).then_inc(row_free[0], 1)
            act.wait_ge(row_full, 2 * i + 2)
            if i >= 2:
                act.wait_ge(row_free[1], i - 1)
            act.activation(sig[0:r, i % 2], PS[0:r, 2 * (i % 2) + 1], ACT.Sigmoid).then_inc(sig_ready, 1)

    @block.vector
    def _(dve):
        own = Steps(dve, own_s)
        dve.wait_ge(small_in, 32)
        m = lb[:, 2]
        own.link(dve.tensor_tensor(m, logits[:, 0], logits[:, 1], ALU.max))
        own.did(dve.tensor_tensor(logits[:, 0], logits[:, 0], m, ALU.subtract))
        own.did(dve.tensor_tensor(logits[:, 1], logits[:, 1], m, ALU.subtract))
        dve.wait_ge(exp_ready, 1)
        own.link(dve.tensor_tensor(m, logits[:, 0], logits[:, 1], ALU.add))
        own.link(dve.reciprocal(m, m))
        own.link(dve.tensor_tensor(lb[:, 0], logits[:, 0], m, ALU.mult))
        own.link(dve.tensor_scalar(lb[:, 1], lb[:, 0], -1.0, 1.0, ALU.mult, ALU.add))
        for h in range(HGH):
            dve.wait_ge(group_free[1], h + 1)
            dve.tensor_scalar(S.hf[:, h], S.hf[:, h], lb[:, 1, h:h + 1], lb[:, 0, h:h + 1], ALU.mult, ALU.add)
        for i in range(NT):
            r = rows(i)
            dve.wait_ge(sig_ready, i + 1)
            own.link(dve.tensor_tensor(sig[0:r, i % 2], sig[0:r, i % 2], S.gain_b[0:r], ALU.mult))
            dve.tensor_tensor(S.hrows[0:r, i, 512:1024], PS[0:r, 2 * (i % 2) + 1], sig[0:r, i % 2], ALU.mult).then_inc(row_free[1], 1)

    S.close(block)
    arena.at = mark


def stage_recurrence(nc, S, I, O):
    arena, PS, sem = S.arena, S.psum, S.sem
    mark = arena.at
    LV = 7
    FULL = NT - 1
    NB = 1 + SAMPLES
    Q, K, A = arena.take(2, HGH * 128), arena.take(2, HGH * 128), arena.take(2, HGH * 128)
    TL = [arena.take(2, HGH * (128 >> l)) for l in range(LV + 1)]
    KR = arena.take(2, HGH * 128)
    state = arena.take(HGH, HGD)
    hg = arena.take(2, HGH * 128)
    ms = arena.take(2, HGH)
    carrier = arena.take(18)
    mask_words = arena.take(LV * HGH * 128 // 4).bitcast(I32)
    masks = mask_words.bitcast(mybir.dt.uint8).rearrange("p (l h t) -> p l h t", l=LV, h=HGH)
    samp = arena.take(SAMPLES, HGH, HGD)
    QZ = arena.take(HGH, NB, LAST)
    KZ = arena.take(NB, HGH * 128)
    bmask = arena.take(NB)
    eye = arena.take(HGH, 128)
    consts, samp_in, state_zero, qz_zero, qz_ready = sem("r_consts"), sem("r_samp"), sem("r_s0"), sem("r_qz0"), sem("r_qz")
    in_ready = [sem("r_in0"), sem("r_in1")]
    lv_full = [sem("r_lf0"), sem("r_lf1")]
    lv_used = [sem("r_lu0"), sem("r_lu1")]
    grown = [sem("r_g0"), sem("r_g1")]
    partial = sem("r_part")
    kr_full, kr_copied, o_full, u_full, s_ready = sem("r_krf"), sem("r_krc"), sem("r_of"), sem("r_uf"), sem("r_sr")
    squared, ms_ready, rooted, rinv_ready, hg_ready, t_full, t_copied = (sem("r_" + x) for x in ("sq", "ms", "rt", "ri", "hg", "tf", "tc"))
    kz_ready, state_out = sem("r_kz"), sem("r_out")

    def h3(v, n=128):
        return v.rearrange("p (h t) -> p h t", h=HGH)[:, :, 0:n]

    block = S.block()

    @block.sync
    def _(sp):
        sp.dma_start(mask_words, I["c_levels"]).then_inc(consts, 16)
        sp.dma_start(eye.rearrange("p h t -> p (h t)"), I["c_eye4"]).then_inc(consts, 16)
        sp.dma_start(bmask[0:LAST], I["c_blocks"]).then_inc(consts, 16)
        sp.dma_start(samp.rearrange("p s h v -> p (s h) v"), I["state_hgrn"][0].rearrange("s h d v -> d (s h) v")).then_inc(samp_in, 16)
        sp.wait_ge(s_ready, FULL + NB)
        sp.dma_start(O[4][0, 0].rearrange("h d v -> d h v"), state).then_inc(state_out, 16)
        sp.dma_start(O[7][0].rearrange("s h d v -> d (s h) v"), samp.rearrange("p s h v -> p (s h) v")).then_inc(state_out, 16)
        sp.wait_ge(state_out, 32)

    @block.gpsimd
    def _(pool):
        pool.memset(state.rearrange("p h v -> p (h v)"), 0.0).then_inc(state_zero, 1)
        pool.memset(QZ.rearrange("p h b t -> p (h b t)"), 0.0).then_inc(qz_zero, 1)
        pool.wait_ge(qz_zero, 1)
        pool.wait_ge(grown[0], 8 * (FULL // 2) + 5)
        for b in range(NB):
            c0, n = (0, TAIL) if b == 0 else (TAIL + NEW * (b - 1), NEW)
            pool.tensor_copy(QZ[:, :, b, c0:c0 + n], h3(Q[:, 0])[:, :, c0:c0 + n]).then_inc(qz_ready, 1)

    @block.tensor
    def _(pe):
        def level(b, done, wait, n=128):
            pe.wait_ge(*wait)
            for h in range(HGH):
                ins = pe.matmul(PS[0:n, b, 128 * h:128 * h + n], K[:, b, 128 * h:128 * h + n], Q[:, b, 128 * h:128 * h + n],
                                start=True, stop=True)
            ins.then_inc(lv_full[b], 1)

        def turn_k(b, c, n=128):
            if c is not None:
                pe.wait_ge(kr_copied, c)
            for h in range(HGH):
                ins = pe.transpose(PS[0:n, 4, 128 * h:128 * (h + 1)], K[:, b, 128 * h:128 * h + n], S.ident)
            ins.then_inc(kr_full, 1)

        def turn_out(b, c, n=128):
            pe.wait_ge(hg_ready, c)
            for h in range(HGH):
                ins = pe.transpose(PS[:, 6, 128 * h:128 * h + n], hg[0:n, b, 128 * h:128 * (h + 1)], S.ident[0:n, 0:n])
            ins.then_inc(t_full, 1)

        pe.wait_ge(state_zero, 1)
        with pe.Fori(0, FULL // 2) as it:
            for l in range(LV + 1):
                for b in range(2):
                    if l == 0:
                        pe.wait_ge(in_ready[b], it + 1)
                    else:
                        pe.wait_ge(lv_used[b], 8 * it + l)
                    level(b, None, (grown[b], 8 * it + l) if l else (in_ready[b], it + 1))
            for b in range(2):
                pe.wait_ge(grown[b], 8 * it + 8)
                if b:
                    pe.wait_ge(kr_copied, 2 * it + 1)
                turn_k(b, None)
            for b in range(2):
                v = S.hrows[:, bass.ds(2 * it + b, 1), 0:512].rearrange("p a v -> p (a v)")
                pe.wait_ge(lv_used[b], 8 * it + 8)
                if b:
                    pe.wait_ge(s_ready, 2 * it + 1)
                for h in range(HGH):
                    cols = slice(128 * h, 128 * (h + 1))
                    pe.matmul(PS[:, 2 + b, cols], A[:, b, cols], S.hrows[:, bass.ds(2 * it + b, 1), 128 * h:128 * (h + 1)], start=True, stop=False)
                    ins = pe.matmul(PS[:, 2 + b, cols], Q[:, b, cols], state[:, h], start=False, stop=True)
                ins.then_inc(o_full, 1)
                pe.wait_ge(kr_copied, 2 * it + b + 1)
                for h in range(HGH):
                    ins = pe.matmul(PS[:, 5, 128 * h:128 * (h + 1)], KR[:, b, 128 * h:128 * (h + 1)],
                                    S.hrows[:, bass.ds(2 * it + b, 1), 128 * h:128 * (h + 1)], start=True, stop=True)
                ins.then_inc(u_full, 1)
            turn_out(0, 2 * it + 1)
            pe.wait_ge(t_copied, 2 * it + 1)
            turn_out(1, 2 * it + 2)
            pe.wait_ge(s_ready, 2 * it + 2)
        n = LAST
        base = 8 * (FULL // 2)
        for l in range(5):
            if l:
                pe.wait_ge(lv_used[0], base + l)
            level(0, None, (grown[0], base + l) if l else (in_ready[0], FULL // 2 + 1), n)
        pe.wait_ge(grown[0], base + 5)
        turn_k(0, FULL, n)
        pe.wait_ge(lv_used[0], base + 5)
        pe.wait_ge(qz_ready, NB)
        pe.wait_ge(samp_in, 16)
        for h in range(HGH):
            cols = slice(128 * h, 128 * (h + 1))
            pe.matmul(PS[0:n, 2, cols], A[0:n, 0, 128 * h:128 * h + n], S.hrows[0:n, FULL, cols], start=True, stop=False)
            for b in range(NB):
                ins = pe.matmul(PS[0:n, 2, cols], QZ[:, h, b], state[:, h] if b == 0 else samp[:, b - 1, h], start=False, stop=(b == NB - 1))
        ins.then_inc(o_full, 1)
        for b in range(NB):
            pe.wait_ge(kz_ready, b + 1)
            if b >= 2:
                pe.wait_ge(s_ready, FULL + b - 1)
            for h in range(HGH):
                cols = slice(128 * h, 128 * (h + 1))
                ins = pe.matmul(PS[:, (5, 7)[b % 2], cols], KZ[0:n, b, cols], S.hrows[0:n, FULL, cols], start=True, stop=True)
            ins.then_inc(u_full, 1)
        pe.wait_ge(t_copied, FULL)
        turn_out(0, FULL + 1, n)

    @block.scalar
    def _(act):
        def bring(b, of, n=128):
            act.copy(h3(Q[:, b], n), of(S.hq))
            act.copy(h3(TL[0][:, b], n), of(S.hf))
            act.activation(h3(K[:, b], n), of(S.hf), ACT.Copy, bias=1.0, scale=-1.0).then_inc(in_ready[b], 1)

        def out_norm(b, c, n=128):
            act.wait_ge(o_full, c)
            for h in range(HGH):
                ins = act.activation(hg[0:n, b, 128 * h:128 * (h + 1)], PS[0:n, 2 + b, 128 * h:128 * (h + 1)], ACT.Square, accum_out=ms[0:n, b, h:h + 1])
            ins.then_inc(squared, 1)
            act.wait_ge(ms_ready, c)
            act.activation(ms[0:n, b], ms[0:n, b], ACT.Sqrt).then_inc(rooted, 1)

        with act.Fori(0, FULL // 2) as it:
            for b in range(2):
                bring(b, lambda v: v[:, :, bass.ds(128 * (2 * it + b), 128)])
            for b in range(2):
                act.wait_ge(kr_full, 2 * it + b + 1)
                act.copy(KR[:, b], PS[:, 4]).then_inc(kr_copied, 1)
            for b in range(2):
                out_norm(b, 2 * it + b + 1)
            for b in range(2):
                act.wait_ge(t_full, 2 * it + b + 1)
                act.copy(carrier[:, 16 + b:17 + b], S.ident[:, 0:1])
                act.copy(S.hq[:, :, bass.ds(128 * (2 * it + b), 128)], h3(PS[:, 6])).then_inc(t_copied, 1)
        n = LAST
        bring(0, lambda v: v[:, :, 128 * FULL:T], n)
        act.wait_ge(kr_full, FULL + 1)
        act.copy(KR[0:n, 0], PS[0:n, 4]).then_inc(kr_copied, 1)
        out_norm(0, FULL + 1, n)
        act.wait_ge(t_full, FULL + 1)
        act.copy(S.hq[:, :, 128 * FULL:T], h3(PS[:, 6], n)).then_inc(t_copied, 1)

    @block.vector
    def _(dve):
        own = Steps(dve, partial)

        def take_level(b, l, full, n=128, only=None):
            dve.wait_ge(lv_full[b], full)
            dve.memset(carrier[:, 2 * l + b:2 * l + b + 1], 0.0)
            a, p = h3(A[0:n, b], n), h3(PS[0:n, b], n)
            if l == 0:
                dve.tensor_tensor(a, p, eye[0:n, :, 0:n], ALU.mult).then_inc(lv_used[b], 1)
            else:
                r = only or n
                dve.copy_predicated(a[0:r, :, 0:r], masks[0:r, l - 1, :, 0:r], p[0:r, :, 0:r]).then_inc(lv_used[b], 1)

        def grow(b, l, n=128):
            q, k = h3(Q[:, b], n), h3(K[:, b], n)
            if l == 0:
                dve.tensor_tensor(q, q, h3(TL[0][:, b], n), ALU.mult).then_inc(grown[b], 1)
                return
            half, w = 1 << (l - 1), HGH * (128 >> (l - 1))
            t = TL[l - 1][:, b].rearrange("p (h m) -> p h m", h=HGH)[:, :, 0:n // half]
            if n == 128:
                tt = TL[l - 1][:, b].rearrange("p (m two) -> p m two", two=2)
                qq = Q[:, b].rearrange("p (m two x) -> p m two x", two=2, x=half)
                kk = K[:, b].rearrange("p (m two x) -> p m two x", two=2, x=half)
                m = w // 2
                dve.tensor_tensor(TL[l][:, b], tt[:, :, 0], tt[:, :, 1], ALU.mult)
                dve.tensor_tensor(qq[:, :, 1], qq[:, :, 1], tt[:, :, 0:1].to_broadcast([128, m, half]), ALU.mult)
                dve.tensor_tensor(kk[:, :, 0], kk[:, :, 0], tt[:, :, 1:2].to_broadcast([128, m, half]), ALU.mult).then_inc(grown[b], 1)
                return
            m = n // (2 * half)
            for h in range(HGH):
                tt = t[:, h].rearrange("p (m two) -> p m two", two=2)
                qq = q[:, h].rearrange("p (m two x) -> p m two x", two=2, x=half)
                kk = k[:, h].rearrange("p (m two x) -> p m two x", two=2, x=half)
                dst = TL[l][:, b].rearrange("p (h m) -> p h m", h=HGH)[:, h, 0:m]
                dve.tensor_tensor(dst, tt[:, :, 0], tt[:, :, 1], ALU.mult)
                dve.tensor_tensor(qq[:, :, 1], qq[:, :, 1], tt[:, :, 0:1].to_broadcast([128, m, half]), ALU.mult)
                ins = dve.tensor_tensor(kk[:, :, 0], kk[:, :, 0], tt[:, :, 1:2].to_broadcast([128, m, half]), ALU.mult)
            ins.then_inc(grown[b], 1)

        def new_state(st, bank, tot, u, last=True):
            dve.wait_ge(u_full, u)
            for h in range(HGH):
                ins = dve.scalar_tensor_tensor(st[:, h], st[:, h], tot(h), PS[:, bank, 128 * h:128 * (h + 1)], ALU.mult, ALU.add)
            ins.then_inc(s_ready, 1)

        def finish(b, c, gate, n=128):
            dve.wait_ge(squared, c)
            dve.tensor_scalar(ms[0:n, b], ms[0:n, b], 1.0 / HGD, EPS, ALU.mult, ALU.add).then_inc(ms_ready, 1)
            dve.wait_ge(rooted, c)
            dve.reciprocal(ms[0:n, b], ms[0:n, b]).then_inc(rinv_ready, 1)
            dve.wait_ge(rinv_ready, c)
            for h in range(HGH):
                ins = dve.scalar_tensor_tensor(hg[0:n, b, 128 * h:128 * (h + 1)], PS[0:n, 2 + b, 128 * h:128 * (h + 1)],
                                               ms[0:n, b, h:h + 1], gate(h), ALU.mult, ALU.mult)
            ins.then_inc(hg_ready, 1)

        dve.wait_ge(consts, 48)
        with dve.Fori(0, FULL // 2) as it:
            for l in range(LV + 1):
                for b in range(2):
                    take_level(b, l, 8 * it + l + 1)
                    if l:
                        dve.wait_ge(grown[b], 8 * it + l)
                    grow(b, l)
            for b in range(2):
                dve.wait_ge(grown[b], 8 * it + 8)
                dve.wait_ge(o_full, 2 * it + b + 1)
                new_state(state, 5, lambda h: TL[LV][:, b, h:h + 1], 2 * it + b + 1)
                finish(b, 2 * it + b + 1, lambda h: S.hrows[:, bass.ds(2 * it + b, 1), 512 + 128 * h:512 + 128 * (h + 1)].rearrange("p a v -> p (a v)"))
        n, base = LAST, 8 * (FULL // 2)
        for l in range(4):
            take_level(0, l, base + l + 1, n)
            if l:
                dve.wait_ge(grown[0], base + l)
            grow(0, l, n)
        take_level(0, 4, base + 5, n, only=TAIL)
        dve.wait_ge(grown[0], base + 4)
        t8 = TL[3][:, 0].rearrange("p (h m) -> p h m", h=HGH)
        q, k = h3(Q[:, 0]), h3(K[:, 0])
        own.did(dve.tensor_tensor(TL[4][:, 0, 0:HGH].rearrange("p (h m) -> p h m", m=1), t8[:, :, 0:1], t8[:, :, 1:2], ALU.mult))
        dve.tensor_tensor(q[:, :, NEW:TAIL], q[:, :, NEW:TAIL], t8[:, :, 0:1].to_broadcast([128, HGH, NEW]), ALU.mult)
        dve.tensor_tensor(k[:, :, 0:NEW], k[:, :, 0:NEW], t8[:, :, 1:2].to_broadcast([128, HGH, NEW]), ALU.mult).then_inc(grown[0], 1)
        dve.wait_ge(kr_copied, FULL + 1)
        for b in range(NB):
            dve.tensor_scalar(KZ[0:n, b], KR[0:n, 0], bmask[0:n, b:b + 1], None, ALU.mult).then_inc(kz_ready, 1)
        own.settle()
        dve.wait_ge(o_full, FULL + 1)
        for b in range(NB):
            st = state if b == 0 else samp[:, b - 1]
            tot = (lambda h: TL[4][:, 0, h:h + 1]) if b == 0 else (lambda h, b=b: t8[:, h, b + 1:b + 2])
            new_state(st, (5, 7)[b % 2], tot, FULL + b + 1)
        finish(0, FULL + 1, lambda h: S.hrows[0:n, FULL, 512 + 128 * h:512 + 128 * (h + 1)], n)

    S.close(block)
    arena.at = mark


def stage_merge(nc, S, I, O):
    arena, PS, sem = S.arena, S.psum, S.sem
    mark = arena.at
    BR = 4
    w = arena.take(2, 2 * (KD + BR), 128)
    sa, sb = arena.take(2, CH), arena.take(2, CH)
    unused = arena.take(2)
    w_in = [sem("m_w0"), sem("m_w1")]
    unit_full, sig_ready, gated, merged_ready, table_set = sem("m_full"), sem("m_sig"), sem("m_gated"), sem("m_ready"), sem("m_table")
    S.wout_in = sem("m_wout")
    U = 2 * NCH

    block = S.block()

    @block.sync
    def _(sp):
        def load(s, cols):
            for at, rows_, c in ((0, I["w_in"][0], C_GA), (KD + BR, I["w_in"][0], C_GB)):
                sp.dma_start(w[:, s, at:at + KD], rows_[:, cols(c)].rearrange("(k p) n -> p k n", p=128)).then_inc(w_in[s], 16)
            for at, rows_ in ((KD, I["w_br_mla"][0]), (2 * KD + BR, I["w_br_hg"][0])):
                sp.dma_start(w[:, s, at:at + BR], rows_[:, cols(0)].rearrange("(k p) n -> p k n", p=128)).then_inc(w_in[s], 16)

        load(0, lambda c: slice(c, c + 128))
        load(1, lambda c: slice(c + 128, c + 256))
        sp.dma_start(S.wout, I["w_out"][0].rearrange("(k p) n -> p k n", p=128)).then_inc(S.wout_in, 16)
        sp.dma_start(S.table, I["c_table"]).then_inc(table_set, 16)
        with sp.Fori(0, KD // 2 - 1) as it:
            for s in range(2):
                sp.wait_ge(unit_full, U * it + NCH * (s + 1))
                load(s, lambda c: bass.ds(c + 128 * (2 * it + 2 + s), 128))
        sp.wait_ge(table_set, 16)

    @block.tensor
    def _(pe):
        with pe.Fori(0, KD // 2) as it:
            for u in range(U):
                s, n = u // NCH, u % NCH
                if n == 0:
                    pe.wait_ge(w_in[s], 64 * (it + 1))
                pe.wait_ge(merged_ready, U * it + u + 1)
                cols = slice(CH * n, CH * (n + 1))
                for b, (at, k, src) in enumerate(((0, KD, S.xT), (KD, BR, S.mlaT), (KD + BR, KD, S.xT), (2 * KD + BR, BR, S.hq))):
                    for j in range(k):
                        ins = pe.matmul(PS[:, 4 * (u % 2) + b, 0:CH], w[:, s, at + j], src[:, j, cols], start=(j == 0), stop=(j == k - 1))
                ins.then_inc(unit_full, 1)

    @block.scalar
    def _(act):
        with act.Fori(0, KD // 2) as it:
            for u in range(U):
                act.wait_ge(unit_full, U * it + u + 1)
                act.wait_ge(merged_ready, U * it + u + 1)
                act.activation(sa[:, u % 2], PS[:, 4 * (u % 2), 0:CH], ACT.Sigmoid)
                act.activation(sb[:, u % 2], PS[:, 4 * (u % 2) + 2, 0:CH], ACT.Sigmoid).then_inc(sig_ready, 1)

    @block.vector
    def _(dve):
        for j in range(2):
            dve.memset(unused[:, j:j + 1], 0.0).then_inc(merged_ready, 1)
        with dve.Fori(0, KD // 2) as it:
            for u in range(U):
                s, n = u // NCH, u % NCH
                dve.wait_ge(sig_ready, U * it + u + 1)
                dve.tensor_tensor(sa[:, u % 2], sa[:, u % 2], PS[:, 4 * (u % 2) + 1, 0:CH], ALU.mult)
                dve.tensor_tensor(sb[:, u % 2], sb[:, u % 2], PS[:, 4 * (u % 2) + 3, 0:CH], ALU.mult).then_inc(gated, 1)
                dve.wait_ge(gated, U * it + u + 1)
                dve.tensor_tensor(S.merged[:, bass.ds(2 * it + s, 1), CH * n:CH * (n + 1)].rearrange("p a t -> p (a t)"),
                                  sa[:, u % 2], sb[:, u % 2], ALU.add).then_inc(merged_ready, 1)

    S.close(block)
    arena.at = mark


def stage_route(nc, S, I, O):
    arena, PS, sem = S.arena, S.psum, S.sem
    mark = arena.at
    wout = S.wout
    x, gb = (S.branches[:, 2 * DM * j:2 * DM * (j + 1)].rearrange("p (a n) -> p a n", a=2) for j in range(2))
    S.w_shared = S.branches[:, 4 * DM:4 * DM + 2 * KD * DEXP].rearrange("p (j k n) -> p j k n", j=2, k=KD)
    shared_in = sem("o_sh")
    wr = arena.take(KD, EXPERTS)
    bias, eoff, one, pid = arena.take(EXPERTS), arena.take(EXPERTS), arena.take(EXPERTS), arena.take(1)
    stats, mv = arena.take(2, 12), arena.take(2, 4)
    score, biased, left, sel, rank, place = (arena.take(2, EXPERTS) for _ in range(6))
    top = arena.take(2, 8)
    sums = arena.take(2, 2)
    spill = arena.take(2, 2 * TOPK, EXPERTS)
    slot = arena.take(2, TOPK)
    slot_i = arena.take(2, TOPK).bitcast(I32)
    entry = arena.take(2, TOPK, 2)
    token = arena.take(NT).bitcast(I32)
    sel_b = arena.take(NT * EXPERTS // 2).bitcast(BF16).rearrange("p (i e) -> p i e", i=NT)
    before, before_b = arena.take(128), arena.take(64).bitcast(BF16)
    ones_b = arena.take(64).bitcast(BF16)
    over = arena.take(KOVER + 1, EXPERTS)
    ob, row0, cols = arena.take(EXPERTS), arena.take(3, EXPERTS), arena.take(8)
    evens = arena.take(32)
    w_in, c_in, bf_ready = sem("o_w"), sem("o_c"), sem("o_bf")
    x_in, x1_out = [sem("o_x0"), sem("o_x1")], sem("o_out")
    mix_full, sum_ready, var_ready, rooted, x1_ready = sem("o_mix"), sem("o_sum"), sem("o_var"), sem("o_root"), sem("o_x1r")
    t_full, t_copied = sem("o_tf"), [sem("o_tc0"), sem("o_tc1")]
    logit_full, score_ready, sel_ready, place_full, entry_ready, scattered = (sem("o_" + n) for n in ("lf", "sr", "sl", "pf", "er", "sc"))
    scattered = [scattered, sem("o_sc1")]
    own_s, count_full, cols_ready, tab_full = sem("o_own"), sem("o_cf"), sem("o_cr"), sem("o_tabf")

    block = S.block()

    @block.sync
    def _(sp):
        sp.dma_start(wr, I["router_w"][0].rearrange("(k p) n -> p k n", p=128)).then_inc(w_in, 16)
        for dst, name in ((gb[:, 0], "ln1_g"), (gb[:, 1], "ln1_b"), (bias, "router_bias"), (eoff, "c_eoff"), (pid, "c_pid"),
                          (token, "c_token"), (before, "c_before"), (evens[0:1], "c_evens"), (S.blocks_i[0:1, :, 0:EXPERTS], "c_main")):
            sp.dma_start(dst, I[name]).then_inc(c_in, 16)
        for i in range(NT):
            if i >= 2:
                sp.wait_ge(sum_ready, i - 1)
            s = x[:, i % 2]
            if i == 0:
                sp.dma_start(s[0:N_META], I["meta_tokens"]).then_inc(x_in[0], 16)
                sp.dma_start(s[N_META:128], I["x_prompt"][0, 0:128 - N_META]).then_inc(x_in[0], 16)
            elif i < NT - 1:
                sp.dma_start(s, I["x_prompt"][0, 128 * i - N_META:128 * (i + 1) - N_META]).then_inc(x_in[i % 2], 16)
            else:
                sp.dma_start(s[0:TAIL], I["x_prompt"][0, SEQ - TAIL:SEQ]).then_inc(x_in[0], 16)
                sp.dma_start(s[TAIL:LAST], I["x_sample"].rearrange("s n d -> (s n) d")).then_inc(x_in[0], 16)
        for j, name in enumerate(("w_sh_gate", "w_sh_up")):
            sp.dma_start(S.w_shared[:, j], I[name][0].rearrange("(k p) n -> p k n", p=128)).then_inc(shared_in, 16)
        for i in range(NT):
            sp.wait_ge(x1_ready, i + 1)
            sp.dma_start(S.x1_dram[128 * i:128 * i + rows(i)], S.x1[0:rows(i), i]).then_inc(x1_out, 16)
        sp.dma_start(S.x1_dram[T:T + 128], S.x1[:, 0]).then_inc(x1_out, 16)
        sp.dma_start(S.x1_dram[T + 128:T + CAP], S.x1[0:CAP - 128, 1]).then_inc(x1_out, 16)
        sp.wait_ge(x1_out, 16 * (NT + 2))
        sp.wait_ge(shared_in, 32)

    @block.gpsimd
    def _(pool):
        for i in range(NT):
            pool.wait_ge(entry_ready, i + 1)
            for k in range(TOPK):
                pool.indirect_dma_start(out=S.table, out_offset=bass.IndirectOffsetOnAxis(ap=slot_i[0:rows(i), i % 2, k:k + 1], axis=0),
                                        in_=entry[0:rows(i), i % 2, k].bitcast(I32), in_offset=None).then_inc(scattered[i % 2], 16)
        pool.wait_ge(scattered[0], 16 * TOPK * ((NT + 1) // 2))
        pool.wait_ge(scattered[1], 16 * TOPK * (NT // 2))

    @block.tensor
    def _(pe):
        def mix(i):
            r = rows(i)
            if i >= 2:
                pe.wait_ge(sum_ready, i - 1)
            for c in range(2):
                for k in range(KD):
                    ins = pe.matmul(PS[0:r, 2 * (i % 2) + c], S.merged[:, k, 128 * i:128 * i + r], wout[:, k, 512 * c:512 * (c + 1)],
                                    start=(k == 0), stop=(k == KD - 1))
            ins.then_inc(mix_full, 1)

        def turn(i):
            r = rows(i)
            pe.wait_ge(x1_ready, i + 1)
            for g in range(2):
                if i:
                    pe.wait_ge(t_copied[g], i)
                for k in range(4):
                    ins = pe.transpose(PS[:, 4 + g, 128 * k:128 * k + r], S.x1[0:r, i, 512 * g + 128 * k:512 * g + 128 * (k + 1)], S.ident[0:r, 0:r])
                ins.then_inc(t_full, 1)

        def route(i):
            r = rows(i)
            pe.wait_ge(t_copied[0], i + 1)
            pe.wait_ge(t_copied[1], i + 1)
            if i:
                pe.wait_ge(score_ready, i)
            for k in range(KD):
                ins = pe.matmul(PS[0:r, 6, 0:EXPERTS], S.xT[:, k, 128 * i:128 * i + r], wr[:, k], start=(k == 0), stop=(k == KD - 1))
            ins.then_inc(logit_full, 1)

        def places(i):
            r = rows(i)
            pe.wait_ge(sel_ready, i + 1)
            if i:
                pe.wait_ge(entry_ready, i)
            for j in range(i):
                pe.matmul(PS[0:r, 7, 0:EXPERTS], ones_b[:, 0:r], sel_b[:, j], start=(j == 0), stop=False)
            pe.matmul(PS[0:r, 7, 0:EXPERTS], before_b[0:r, 0:r], sel_b[0:r, i], start=(i == 0), stop=True).then_inc(place_full, 1)

        def shared_gate(n):
            for k in range(KD):
                pe.matmul(PS[:, n, 0:CH], S.w_shared[:, 0, k, 0:128], S.xT[:, k, CH * n:CH * (n + 1)], start=(k == 0), stop=(k == KD - 1))

        pe.wait_ge(S.wout_in, 16)
        for i in range(NT + 2):
            if i < NT:
                mix(i)
            if i == NT:
                pe.wait_ge(shared_in, 32)
                pe.wait_ge(sum_ready, NT)
                shared_gate(0)
                shared_gate(1)
            if i == NT + 1:
                shared_gate(2)
            if 1 <= i <= NT:
                turn(i - 1)
            if i == 2:
                pe.wait_ge(bf_ready, 2)
            if i >= 2:
                places(i - 2)
            if 1 <= i <= NT:
                if i == 1:
                    pe.wait_ge(w_in, 16)
                route(i - 1)
        for j in range(NT):
            r = rows(j)
            if j == 0:
                pe.wait_ge(score_ready, NT)
            ins = pe.matmul(PS[:, 6, 0:EXPERTS], ones_b[0:r], sel_b[0:r, j], start=(j == 0), stop=(j == NT - 1))
        ins.then_inc(count_full, 1)
        pe.wait_ge(cols_ready, 1)
        for c in range(2):
            ins = pe.transpose(PS[0:1, 3, 128 * c:128 * (c + 1)], cols[:, c:c + 1], S.ident)
        ins.then_inc(tab_full, 1)

    def copy_back(eng, g, i, copy):
        eng.wait_ge(t_full, 2 * i + g + 1)
        copy(S.xT[:, 4 * g:4 * g + 4, 128 * i:128 * i + rows(i)],
             PS[:, 4 + g].rearrange("p (k t) -> p k t", k=4)[:, :, 0:rows(i)]).then_inc(t_copied[g], 1)

    @block.scalar
    def _(act):
        for i in range(NT + 1):
            if i:
                copy_back(act, 0, i - 1, act.copy)
            if i < NT:
                r = rows(i)
                act.wait_ge(var_ready, i + 1)
                act.activation(mv[0:r, i % 2, 1:2], mv[0:r, i % 2, 1:2], ACT.Sqrt).then_inc(rooted, 1)
            if i:
                r = rows(i - 1)
                act.wait_ge(logit_full, i)
                if i > 2:
                    act.wait_ge(entry_ready, i - 2)
                act.activation(score[0:r, (i - 1) % 2], PS[0:r, 6, 0:EXPERTS], ACT.Sigmoid).then_inc(score_ready, 1)

    @block.vector
    def _(dve):
        own = Steps(dve, own_s)
        dve.wait_ge(c_in, 16 * 9)
        dve.tensor_copy(before_b, before).then_inc(bf_ready, 1)
        dve.memset(ones_b, 1.0).then_inc(bf_ready, 1)
        own.link(dve.memset(one, 1.0))

        def norm(i):
            r, s = rows(i), i % 2
            y = S.x1[0:r, i]
            dve.wait_ge(mix_full, i + 1)
            dve.wait_ge(x_in[s], {0: 32, 8: 112}.get(i, 16 * (i // 2 + 1 + (1 - s))))
            dve.scalar_tensor_tensor(y, x[0:r, s], ALPHA, PS[0:r, 2 * s:2 * s + 2].rearrange("p b c -> p (b c)"),
                                     ALU.mult, ALU.add).then_inc(sum_ready, 1)
            dve.wait_ge(sum_ready, i + 1)
            own.did(dve.bn_stats(stats[0:r, s, 0:6], y[:, 0:512]))
            own.link(dve.bn_stats(stats[0:r, s, 6:12], y[:, 512:1024]))
            own.link(dve.bn_aggr(mv[0:r, s, 0:2], stats[0:r, s]))
            dve.tensor_scalar(mv[0:r, s, 1:2], mv[0:r, s, 1:2], EPS, None, ALU.add).then_inc(var_ready, 1)
            dve.wait_ge(rooted, i + 1)
            own.link(dve.reciprocal(mv[0:r, s, 2:3], mv[0:r, s, 1:2]))
            own.link(dve.tensor_scalar(y, y, mv[0:r, s, 0:1], mv[0:r, s, 2:3], ALU.subtract, ALU.mult))
            own.link(dve.tensor_tensor(y, y, gb[0:r, 0], ALU.mult))
            dve.tensor_tensor(y, y, gb[0:r, 1], ALU.add).then_inc(x1_ready, 1)

        def choose(i):
            r, s = rows(i), i % 2
            dve.wait_ge(score_ready, i + 1)
            if i >= 2:
                dve.wait_ge(scattered[s], 16 * TOPK * (i // 2))
            own.link(dve.tensor_tensor(biased[0:r, s], score[0:r, s], bias[0:r], ALU.add))
            own.link(dve.max(top[0:r, s], biased[0:r, s]))
            own.link(dve.match_replace(left[0:r, s], top[0:r, s], biased[0:r, s], -3e38))
            own.link(dve.tensor_tensor(sel[0:r, s], left[0:r, s], biased[0:r, s], ALU.not_equal))
            dve.tensor_copy(sel_b[0:r, i], sel[0:r, s]).then_inc(sel_ready, 1)
            own.did(dve.tensor_tensor_scan(rank[0:r, s], one[0:r], sel[0:r, s], 0.0, ALU.mult, ALU.add))
            own.link(dve.scalar_tensor_tensor(left[0:r, s], score[0:r, s], 1.0, sel[0:r, s], ALU.mult, ALU.mult, accum_out=sums[0:r, s, 0:1]))
            own.did(dve.tensor_tensor(rank[0:r, s], rank[0:r, s], sel[0:r, s], ALU.mult))
            own.link(dve.reciprocal(sums[0:r, s, 1:2], sums[0:r, s, 0:1]))
            own.link(dve.tensor_scalar(left[0:r, s], left[0:r, s], sums[0:r, s, 1:2], ROUTED_SCALE, ALU.mult, ALU.mult))

        def enter(i):
            r, s = rows(i), i % 2
            dve.wait_ge(place_full, i + 1)
            own.link(dve.tensor_tensor(place[0:r, s], PS[0:r, 7, 0:EXPERTS], eoff[0:r], ALU.add))
            own.settle()
            for k in range(TOPK):
                own.did(dve.scalar_tensor_tensor(spill[0:r, s, k], rank[0:r, s], float(k + 1), place[0:r, s], ALU.is_equal, ALU.mult,
                                                 accum_out=slot[0:r, s, k:k + 1]))
                own.did(dve.scalar_tensor_tensor(spill[0:r, s, TOPK + k], rank[0:r, s], float(k + 1), left[0:r, s], ALU.is_equal, ALU.mult,
                                                 accum_out=entry[0:r, s, k, 1:2]))
            own.did(dve.tensor_copy(entry[0:r, s, :, 0].bitcast(I32), token[0:r, i:i + 1].to_broadcast([r, TOPK])))
            own.settle()
            dve.tensor_copy(slot_i[0:r, s], slot[0:r, s]).then_inc(entry_ready, 1)

        for i in range(NT + 2):
            if 1 <= i <= NT:
                copy_back(dve, 1, i - 1, dve.tensor_copy)
            if i < NT:
                norm(i)
            if i >= 2:
                enter(i - 2)
            if 1 <= i <= NT:
                choose(i - 1)

        dve.wait_ge(count_full, 1)
        own.link(dve.tensor_scalar(over[:, 0], PS[:, 6, 0:EXPERTS], float(CAP), None, ALU.is_gt))
        for k in range(1, KOVER):
            own.link(dve.scalar_tensor_tensor(over[:, k], PS[:, 6, 0:EXPERTS], float(CAP * (k + 1)), over[:, k - 1], ALU.is_gt, ALU.add))
        n_over = over[:, KOVER - 1]
        own.link(dve.tensor_tensor_scan(ob, one, n_over, 0.0, ALU.mult, ALU.add))
        own.did(dve.scalar_tensor_tensor(row0[:, 0], ob, pid, one, ALU.is_le, ALU.mult, accum_out=cols[:, 2:3]))
        own.link(dve.scalar_tensor_tensor(row0[:, 1], ob, pid, n_over, ALU.is_le, ALU.mult, accum_out=cols[:, 3:4]))
        own.did(dve.tensor_scalar(cols[:, 0:1], cols[:, 2:3], float(EXPERTS - 1), None, ALU.min))
        own.link(dve.tensor_tensor(cols[:, 4:5], pid, cols[:, 3:4], ALU.subtract))
        own.link(dve.tensor_scalar(cols[:, 5:6], cols[:, 4:5], float(CAP), float(CAP), ALU.mult, ALU.add))
        own.link(dve.scalar_tensor_tensor(cols[:, 6:7], cols[:, 2:3], float(VCAP), cols[:, 5:6], ALU.mult, ALU.add))
        dve.tensor_scalar(cols[:, 1:2], cols[:, 6:7], float(EXPERTS * VCAP), None, ALU.min).then_inc(cols_ready, 1)
        own.link(dve.scalar_tensor_tensor(row0[0:1, 2, 0:32], evens[0:1], ob[0:1, EXPERTS - 1:EXPERTS], one[0:1, 0:32], ALU.is_lt, ALU.mult,
                                          accum_out=cols[0:1, 7:8]))
        own.link(dve.tensor_scalar(cols[0:1, 7:8], cols[0:1, 7:8], float(EXPERTS // 2 - 1), None, ALU.add))
        own.did(dve.tensor_copy(S.pairs_i[0:1], cols[0:1, 7:8]))
        dve.wait_ge(tab_full, 1)
        own.link(dve.tensor_copy(S.blocks_i[0:1, :, EXPERTS:2 * EXPERTS], PS[0:1, 3, 0:256].rearrange("p (a b) -> p a b", a=2)[:, :, 0:EXPERTS]))

    S.close(block)
    arena.at = mark


def stage_shared(nc, S, I, O):
    arena, PS, sem = S.arena, S.psum, S.sem
    mark = arena.at
    w = S.w_shared
    wd = arena.take(2, DM)
    hT = arena.take(2, T)
    sg = arena.take(T)
    y = arena.take(3, DM)
    wd_in, full, gate_free = sem("d_wd"), sem("d_full"), sem("d_free")
    sig_ready, h_own, h_ready, row_full, y_ready, y_out = (sem("d_" + n) for n in ("sg", "ho", "hr", "rf", "yr", "yo"))
    y_out = [y_out, sem("d_yo1"), sem("d_yo2")]

    def bank3(g):
        return PS[:, 3 * (g % 2):3 * (g % 2) + NCH, 0:CH]

    def col3(v):
        return v.rearrange("p (n c) -> p n c", n=NCH)

    block = S.block()

    @block.sync
    def _(sp):
        sp.dma_start(wd, I["w_sh_down"][0].rearrange("(k p) n -> p k n", p=128)).then_inc(wd_in, 16)
        for i in range(NT):
            sp.wait_ge(y_ready, i + 1)
            src = y[0:rows(i), i % 3]
            sp.dma_start(S.y_dram[128 * i:128 * i + rows(i)], src).then_inc(y_out[i % 3], 16)
            if i < 2:
                n = 128 if i == 0 else CAP - 128
                sp.dma_start(S.y_dram[T + 128 * i:T + 128 * i + n], y[0:n, i]).then_inc(y_out[i], 16)
        for j, n in enumerate((4, 4, 3)):
            sp.wait_ge(y_out[j], 16 * n)

    @block.tensor
    def _(pe):
        for g in range(1, 4):
            f, j = g // 2, g % 2
            if g == 2:
                pe.wait_ge(gate_free, 1)
            if g == 3:
                pe.wait_ge(h_ready, 1)
            for n in range(NCH):
                for k in range(KD):
                    ins = pe.matmul(bank3(g)[:, n], w[:, j, k, 128 * f:128 * (f + 1)], S.xT[:, k, CH * n:CH * (n + 1)],
                                    start=(k == 0), stop=(k == KD - 1))
            ins.then_inc(full, 1)
        pe.wait_ge(wd_in, 16)
        pe.wait_ge(h_ready, 2)
        for i in range(NT):
            r = rows(i)
            if i >= 4:
                pe.wait_ge(y_ready, i - 3)
            for c in range(2):
                for f in range(2):
                    ins = pe.matmul(PS[0:r, 2 * (i % 4) + c], hT[:, f, 128 * i:128 * i + r], wd[:, f, 512 * c:512 * (c + 1)],
                                    start=(f == 0), stop=(f == 1))
            ins.then_inc(row_full, 1)

    @block.scalar
    def _(act):
        for f in range(2):
            if f:
                act.wait_ge(full, 2)
                act.wait_ge(h_ready, 1)
            act.activation(col3(sg), bank3(0), ACT.Sigmoid).then_inc(sig_ready, 1)

    @block.vector
    def _(dve):
        for f in range(2):
            dve.wait_ge(sig_ready, f + 1)
            dve.tensor_tensor(col3(sg), col3(sg), bank3(0), ALU.mult).then_inc(gate_free, 1)
            dve.wait_ge(gate_free, f + 1)
            dve.wait_ge(full, 2 * f + 1)
            dve.tensor_tensor(col3(hT[:, f]), col3(sg), bank3(1), ALU.mult).then_inc(h_ready, 1)
        for i in range(NT):
            r = rows(i)
            dve.wait_ge(row_full, i + 1)
            if i >= 3:
                dve.wait_ge(y_out[i % 3], 16 * (i // 3 + (1 if i % 3 < 2 else 0)))
            dve.scalar_tensor_tensor(y[0:r, i % 3], S.x1[0:r, i], ALPHA, PS[0:r, 2 * (i % 4):2 * (i % 4) + 2].rearrange("p b c -> p (b c)"),
                                     ALU.mult, ALU.add).then_inc(y_ready, 1)

    S.close(block)
    arena.at = mark


def stage_experts(nc, S, I, O):
    arena, split, PS, sem = S.arena, S.split, S.psum, S.sem
    mark = arena.at
    raw = arena.take(2, 3, 2 * DM)
    xg = arena.take(2, 2, DM)
    g32, u32, sg, h32 = (arena.take(2, CAP) for _ in range(4))
    y = arena.take(2, 2, DM)
    gi, si = arena.take(2, 4), arena.take(2, 4)
    spare = arena.take(8)
    wr = split.take(2, 3, 2, 2 * DM)
    xr = split.take(2, 2 * KD, HALF)
    hr = split.take(2, 2, CAP + 128 - HALF)
    raw_in = [[sem(f"e_{n}{s}") for s in range(2)] for n in ("wg", "wu", "wd")]
    gi_in, si_in, xg_in, y_out = ([sem(f"e_{n}{s}") for s in range(2)] for n in ("gi", "si", "xg", "yo"))
    rounded, parted = ([sem(f"e_{n}{j}") for j in range(3)] for n in ("hi", "lo"))
    xr_full, xr_rounded, xr_parted = sem("e_xrf"), sem("e_xrh"), [sem("e_xrl0"), sem("e_xrl1")]
    gate_full, up_full, sig_ready, gated, h_made, h_ready = (sem("e_" + n) for n in ("gf", "uf", "sg", "gg", "hm", "hr"))
    gate_half, up_half, gate_ready, up_ready = (sem("e_" + n) for n in ("gh", "uh", "gr", "ur"))
    part_full, part_copied, zeros = sem("e_pf"), sem("e_pc"), sem("e_zero")
    si_free = [sem("e_sf0"), sem("e_sf1")]
    passed = sem("e_passed")
    GBANK, UBANK, DBANK = (2, 3), (4, 5), (6, 7)
    HI, LO = 0, 1
    GATE, UP, DOWN = 0, 1, 2

    def last_pair(eng):
        return eng.value_load(S.pairs_i[0:1, 0:1], min_val=EXPERTS // 2 - 1, max_val=NBLK_MAX // 2 - 1)

    def quarter(v, hf, g):
        return v[:, KD * hf + 4 * g:KD * hf + 4 * (g + 1)]

    def bank4(g):
        return PS[:, g, 0:4 * HALF].rearrange("p (k t) -> p k t", k=4)

    block = S.block()

    @block.sync
    def _(sp):
        last = last_pair(sp)

        def first_slot(n):
            return sp.value_load(S.blocks_i[0:1, 1, bass.ds(n, 1)], min_val=0, max_val=SLOTS - CAP)

        def expert(n):
            return sp.value_load(S.blocks_i[0:1, 0, bass.ds(n, 1)], min_val=0, max_val=EXPERTS - 1)

        def entries(dst, sems, s, first):
            sp.dma_start(dst[0:HALF, s].rearrange("p (h w) -> p h w", h=2).bitcast(I32),
                         S.table[bass.ds(first, CAP)].rearrange("(h p) w -> p h w", p=HALF)).then_inc(sems[s], 16)

        def weights(s, j, e):
            name = ("w_exp_gate", "w_exp_up", "w_exp_down")[j]
            src = I[name][0, bass.ds(e, 1)].rearrange("a (k p) n -> p (a k) n", p=128)
            sp.dma_start(raw[:, s, j].rearrange("p (k n) -> p k n", k=KD if j < DOWN else 2), src).then_inc(raw_in[j][s], 16)

        for s in range(2):
            entries(gi, gi_in, s, first_slot(s))
        for s in range(2):
            for j in range(3):
                if s == 0 and j == 1:
                    sp.wait_ge(xg_in[0], 32)
                weights(s, j, s)
        with sp.Fori(0, last) as it:
            first = [first_slot(2 * it + s) for s in range(4)]
            e = [expert(2 * it + 2 + s) for s in range(2)]
            for s in range(2):
                n = 2 * it + s
                sp.wait_ge(xg_in[s], 32 * (it + 1))
                entries(gi, gi_in, s, first[2 + s])
                for j in range(3):
                    sp.wait_ge(parted[j], n + 1)
                    weights(s, j, e[s])
                sp.wait_ge(si_free[s], it + 1)
                entries(si, si_in, s, first[s])
        ends = [first_slot(2 * last + s) for s in range(2)]
        for s in range(2):
            sp.wait_ge(si_free[s], last + 1)
            entries(si, si_in, s, ends[s])

    @block.gpsimd
    def _(pool):
        last = last_pair(pool)

        def gather(s, turn):
            pool.wait_ge(gi_in[s], 16 * (turn + 1))
            pool.sem_inc(passed, 1)
            for hf in range(2):
                pool.indirect_dma_start(out=xg[0:HALF, s, hf], out_offset=None, in_=S.x1_dram,
                                        in_offset=bass.IndirectOffsetOnAxis(ap=gi[0:HALF, s, 2 * hf:2 * hf + 1].bitcast(I32), axis=0)
                                        ).then_inc(xg_in[s], 16)

        def scatter(s, turn):
            if s:
                pool.wait_ge(y_out[0], 32 * (turn + 1))
                pool.sem_inc(si_free[0], 1)
            pool.wait_ge(part_copied, 4 * (2 * turn + s) + 8)
            pool.sem_inc(passed, 1)
            for hf in range(2):
                pool.indirect_dma_start(out=S.y_dram, in_=y[0:HALF, s, hf], in_offset=None, compute_op=ALU.add,
                                        out_offset=bass.IndirectOffsetOnAxis(ap=si[0:HALF, s, 2 * hf:2 * hf + 1].bitcast(I32), axis=0)
                                        ).then_inc(y_out[s], 16)

        def body(it, ends):
            for s in range(2):
                if not ends:
                    pool.wait_ge(xr_full, 4 * (2 * it + s + 1))
                    gather(s, it + 1)
                scatter(s, it)
            pool.wait_ge(y_out[1], 32 * (it + 1))
            pool.sem_inc(si_free[1], 1)

        for s in range(2):
            pool.sem_inc(si_free[s], 1)
        gather(0, 0)
        gather(1, 0)
        with pool.Fori(0, last) as it:
            body(it, False)
        body(last, True)

    @block.tensor
    def _(pe):
        last = last_pair(pe)

        def turn(s, turn_, r, first=False):
            n = 2 * turn_ + s
            hf, g = r // 2, r % 2
            if r == 0:
                pe.wait_ge(xg_in[s], 32 * (turn_ + 1))
            if not (first and r < 2):
                pe.wait_ge(xr_parted[g], 2 * n + hf)
            for k in range(4):
                ins = pe.transpose(PS[:, g, HALF * k:HALF * (k + 1)], xg[0:HALF, s, hf, 512 * g + 128 * k:512 * g + 128 * (k + 1)],
                                   S.ident[0:HALF, 0:HALF])
            ins.then_inc(xr_full, 1)

        def gate_up(s, turn_):
            n = 2 * turn_ + s
            for g in range(2):
                pe.wait_ge(xr_parted[g], 2 * n + 2)
            x = xr.rearrange("p c (h k) t -> p k (c h) t", h=2)
            for j, banks in enumerate((GBANK, UBANK)):
                pe.wait_ge(parted[j], n + 1)
                for f in range(2):
                    for k in range(KD):
                        at = DEXP * k + 128 * f
                        if k == 0:
                            pe.matmul(PS[:, banks[f], 0:2 * CAP], wr[:, s, j, HI, at:at + 128], x[:, k], start=True, stop=False)
                        ins = pe.matmul(PS[:, banks[f], 0:CAP], wr[:, s, j, LO, at:at + 128], x[:, k, 0:2], start=False, stop=False)
                        if k > 0:
                            ins = pe.matmul(PS[:, banks[f], 0:2 * CAP], wr[:, s, j, HI, at:at + 128], x[:, k], start=False, stop=(k == KD - 1))
                    if j == UP:
                        ins.then_inc(up_full, 1)
                    elif f == 1:
                        ins.then_inc(gate_full, 1)

        def down(s, turn_, p, f):
            n = 2 * turn_ + s
            hf, c = p // 2, p % 2
            if p == 0 and f == 0:
                pe.wait_ge(parted[DOWN], n + 1)
            if f == 0:
                pe.wait_ge(part_copied, 4 * n + p + 3)
            at = DM * f + 512 * c
            for j, (a, b) in enumerate(((HI, HI), (HI, LO), (LO, HI))):
                if p == 0 and j == 0:
                    pe.wait_ge(h_made, 4 * n + 2 * f + 1)
                if p == 0 and j == 2:
                    pe.wait_ge(h_ready, 2 * n + f + 1)
                ins = pe.matmul(PS[:, DBANK[c]], hr[:, a, f, HALF * hf:HALF * hf + 128], wr[:, s, DOWN, b, at:at + 512],
                                start=(f == 0 and j == 0), stop=(f == 1 and j == 2))
            if f == 1:
                ins.then_inc(part_full, 1)

        def body(it, ends):
            for s in range(2):
                gate_up(s, it)
                more = not (ends and s)
                nxt = (1, it) if s == 0 else (0, it + 1)
                if more:
                    turn(*nxt, 0)
                    turn(*nxt, 1)
                down(s, it, 0, 0)
                down(s, it, 1, 0)
                down(s, it, 0, 1)
                if more:
                    turn(*nxt, 2)
                down(s, it, 1, 1)
                for p in (2, 3):
                    if more and p == 2:
                        turn(*nxt, 3)
                    for f in range(2):
                        down(s, it, p, f)

        for r in range(4):
            turn(0, 0, r, first=True)
        pe.wait_ge(zeros, 4)
        with pe.Fori(0, last) as it:
            body(it, False)
        body(last, True)

    @block.scalar
    def _(act):
        last = last_pair(act)

        def round_weights(s, turn_, j):
            act.wait_ge(raw_in[j][s], 16 * (turn_ + 1))
            act.copy(wr[:, s, j, HI], raw[:, s, j]).then_inc(rounded[j], 1)

        def round_quarter(s, turn_, r):
            hf, g = r // 2, r % 2
            act.wait_ge(xr_full, 4 * (2 * turn_ + s) + r + 1)
            act.copy(quarter(xr[:, HI], hf, g), bank4(g)).then_inc(xr_rounded, 1)

        def part(s, turn_, p):
            hf, c = p // 2, p % 2
            if p == 0:
                act.wait_ge(si_in[s], 16 * (turn_ + 1))
            act.wait_ge(part_full, 4 * (2 * turn_ + s) + p + 1)
            act.activation(y[0:HALF, s, hf, 512 * c:512 * (c + 1)], PS[0:HALF, DBANK[c]], ACT.Copy,
                           scale=si[0:HALF, s, 2 * hf + 1:2 * hf + 2]).then_inc(part_copied, 1)

        def body(it, ends):
            for s in range(2):
                nxt = (1, it) if s == 0 else (0, it + 1)
                more = not (ends and s)
                if more:
                    round_weights(*nxt, GATE)
                    round_weights(*nxt, DOWN)
                act.wait_ge(gate_full, 2 * it + s + 1)
                act.copy(g32, PS[:, GBANK[0]:GBANK[1] + 1, CAP:2 * CAP]).then_inc(gate_half, 1)
                act.wait_ge(gate_ready, 2 * it + s + 1)
                act.activation(sg, g32, ACT.Sigmoid).then_inc(sig_ready, 1)
                for f in range(2):
                    act.wait_ge(up_full, 2 * (2 * it + s) + f + 1)
                    act.copy(u32[:, f], PS[:, UBANK[f], CAP:2 * CAP]).then_inc(up_half, 1)
                    if more and f == 0:
                        round_weights(*nxt, UP)
                if more:
                    round_quarter(*nxt, 0)
                for p in range(4):
                    if more and p < 3:
                        round_quarter(*nxt, p + 1)
                    part(s, it, p)

        round_weights(0, 0, GATE)
        for r in range(4):
            round_quarter(0, 0, r)
        round_weights(0, 0, UP)
        round_weights(0, 0, DOWN)
        for j in range(4):
            act.copy(spare[:, j:j + 1], S.ident[:, 0:1]).then_inc(part_copied, 1)
        with act.Fori(0, last) as it:
            body(it, False)
        body(last, True)

    @block.vector
    def _(dve):
        last = last_pair(dve)

        def part_weights(s, turn_, j):
            dve.wait_ge(rounded[j], 2 * turn_ + s + 1)
            dve.tensor_tensor(wr[:, s, j, LO], raw[:, s, j], wr[:, s, j, HI].bitcast(F32), ALU.subtract).then_inc(parted[j], 1)

        def part_quarter(s, turn_, r):
            hf, g = r // 2, r % 2
            dve.wait_ge(xr_rounded, 4 * (2 * turn_ + s) + r + 1)
            dve.tensor_tensor(quarter(xr[:, LO], hf, g), bank4(g), quarter(xr[:, HI], hf, g).bitcast(F32), ALU.subtract).then_inc(xr_parted[g], 1)

        def body(it, ends):
            for s in range(2):
                n = 2 * it + s
                nxt = (1, it) if s == 0 else (0, it + 1)
                more = not (ends and s)
                part_weights(s, it, DOWN)
                if more:
                    part_weights(*nxt, GATE)
                dve.wait_ge(gate_half, n + 1)
                dve.tensor_tensor(g32, g32, PS[:, GBANK[0]:GBANK[1] + 1, 0:CAP], ALU.add).then_inc(gate_ready, 1)
                dve.wait_ge(sig_ready, n + 1)
                dve.tensor_tensor(sg, sg, g32, ALU.mult).then_inc(gated, 1)
                dve.wait_ge(gated, n + 1)
                for f in range(2):
                    dve.wait_ge(up_half, 2 * n + f + 1)
                    dve.tensor_tensor(u32[:, f], u32[:, f], PS[:, UBANK[f], 0:CAP], ALU.add).then_inc(up_ready, 1)
                    dve.wait_ge(up_ready, 2 * n + f + 1)
                    dve.tensor_tensor(hr[:, HI, f, 0:CAP], sg[:, f], u32[:, f], ALU.mult).then_inc(h_made, 1)
                    dve.tensor_tensor(h32[:, f], sg[:, f], u32[:, f], ALU.mult).then_inc(h_made, 1)
                    dve.wait_ge(h_made, 4 * n + 2 * f + 2)
                    dve.tensor_tensor(hr[:, LO, f, 0:CAP], h32[:, f], hr[:, HI, f, 0:CAP].bitcast(F32), ALU.subtract).then_inc(h_ready, 1)
                if more:
                    for r in range(4):
                        part_quarter(*nxt, r)
                        if r == 1:
                            part_weights(*nxt, UP)

        for part in range(2):
            for f in range(2):
                dve.tensor_scalar(hr[:, part, f, CAP:], S.ident[:, 0:128 - HALF], 0.0, None, ALU.mult).then_inc(zeros, 1)
        part_weights(0, 0, GATE)
        for r in range(4):
            part_quarter(0, 0, r)
        part_weights(0, 0, UP)
        with dve.Fori(0, last) as it:
            body(it, False)
        body(last, True)

    S.close(block)
    arena.at = mark


def stage_out(nc, S, I, O):
    arena, PS, sem = S.arena, S.psum, S.sem
    mark = arena.at
    y = arena.take(NT, DM)
    gb = arena.take(2, DM)
    stats, mv = arena.take(NT, 12), arena.take(NT, 4)
    y_in = [sem(f"z_in{i}") for i in range(NT)]
    gb_in, var_ready, rooted, scaled, done, out, own_s = (sem("z_" + n) for n in ("gb", "vr", "rt", "sc", "dn", "out", "own"))
    shift_ready, normed = sem("z_sh"), sem("z_nm")

    block = S.block()

    @block.sync
    def _(sp):
        for i in range(NT):
            sp.dma_start(y[0:rows(i), i], S.y_dram[128 * i:128 * i + rows(i)]).then_inc(y_in[i], 16)
        sp.dma_start(gb[:, 0], I["ln2_g"]).then_inc(gb_in, 16)
        sp.dma_start(gb[:, 1], I["ln2_b"]).then_inc(gb_in, 16)
        for i in range(NT):
            sp.wait_ge(done, i + 1)
            if i == 0:
                sp.dma_start(O[0][0, 0:128 - N_META], y[N_META:128, 0]).then_inc(out, 16)
            elif i < NT - 1:
                sp.dma_start(O[0][0, 128 * i - N_META:128 * (i + 1) - N_META], y[:, i]).then_inc(out, 16)
            else:
                sp.dma_start(O[0][0, SEQ - TAIL:SEQ], y[0:TAIL, i]).then_inc(out, 16)
                sp.dma_start(O[1].rearrange("s n d -> (s n) d"), y[TAIL:LAST, i]).then_inc(out, 16)
        sp.wait_ge(out, 16 * (NT + 1))

    @block.scalar
    def _(act):
        def root(i):
            act.wait_ge(var_ready, i + 1)
            act.activation(mv[0:rows(i), i, 1:2], mv[0:rows(i), i, 1:2], ACT.Sqrt).then_inc(rooted, 1)

        root(0)
        for i in range(NT):
            r = rows(i)
            if i + 1 < NT:
                root(i + 1)
            act.wait_ge(shift_ready, i + 1)
            act.activation(y[0:r, i], y[0:r, i], ACT.Identity, scale=mv[0:r, i, 2:3], bias=mv[0:r, i, 3:4]).then_inc(normed, 1)

    @block.gpsimd
    def _(pool):
        pool.wait_ge(gb_in, 32)
        for i in range(NT):
            r = rows(i)
            pool.wait_ge(scaled, i + 1)
            pool.tensor_tensor(y[0:r, i], y[0:r, i], gb[0:r, 1], ALU.add).then_inc(done, 1)

    @block.vector
    def _(dve):
        own = Steps(dve, own_s)

        def moments(i):
            r = rows(i)
            dve.wait_ge(y_in[i], 16)
            own.did(dve.bn_stats(stats[0:r, i, 0:6], y[0:r, i, 0:512]))
            own.link(dve.bn_stats(stats[0:r, i, 6:12], y[0:r, i, 512:1024]))
            own.link(dve.bn_aggr(mv[0:r, i, 0:2], stats[0:r, i]))
            dve.tensor_scalar(mv[0:r, i, 1:2], mv[0:r, i, 1:2], EPS, None, ALU.add).then_inc(var_ready, 1)

        def gain(i):
            r = rows(i)
            dve.wait_ge(normed, i + 1)
            dve.tensor_tensor(y[0:r, i], y[0:r, i], gb[0:r, 0], ALU.mult).then_inc(scaled, 1)

        moments(0)
        for i in range(NT):
            r = rows(i)
            if i + 1 < NT:
                moments(i + 1)
            dve.wait_ge(rooted, i + 1)
            own.link(dve.reciprocal(mv[0:r, i, 2:3], mv[0:r, i, 1:2]))
            dve.tensor_scalar(mv[0:r, i, 3:4], mv[0:r, i, 0:1], mv[0:r, i, 2:3], -1.0, ALU.mult, ALU.mult).then_inc(shift_ready, 1)
            if i == 0:
                dve.wait_ge(gb_in, 32)
            else:
                gain(i - 1)
        gain(NT - 1)

    S.close(block)
    arena.at = mark


class State:

    def __init__(self, nc, ctx):
        self.nc, self.ctx = nc, ctx
        self.base = Arena(ctx.enter_context(nc.sbuf_tensor("base", [128, BASE], F32)), BASE)
        self.parts = ctx.enter_context(ExitStack())
        self.big = self.parts.enter_context(nc.sbuf_tensor("big", [128, ARENA], F32))
        self.psum = ctx.enter_context(nc.psum_tensor("banks", [128, 8, 512], F32))
        self.arena = Arena(self.big, ARENA)
        self.sems = []

    def sem(self, name):
        self.sems.append(self.nc.alloc_semaphore(name))
        return self.sems[-1]

    def repart(self):
        self.parts.close()
        self.split = Arena(self.parts.enter_context(self.nc.sbuf_tensor("split", [128, SPLIT], F32R)), SPLIT)
        self.big = self.parts.enter_context(self.nc.sbuf_tensor("rest", [128, ARENA - SPLIT], F32))
        self.arena = Arena(self.big, ARENA - SPLIT)

    def recycle(self):
        self.nc.clear_and_free_semaphores(self.sems)
        self.nc.all_engine_barrier()
        self.sems = []

    def block(self):
        self.open = self.nc.Block()
        return self.open.__enter__()

    def close(self, block):
        self.open.__exit__(None, None, None)


BASE = 128 + 64 + 4 * EXPERTS + 8
ARENA = 53200 - BASE
SPLIT = 2 * 3 * 2 * 2 * DM + 2 * 2 * KD * HALF + 4 * (CAP + 128 - HALF)


def build(nc, I, O):
    with ExitStack() as ctx:
        S = State(nc, ctx)
        a = S.arena
        S.ident = S.base.take(128)
        S.ident_b = S.base.take(64).bitcast(BF16)
        S.blocks_i = S.base.take(2, 2 * EXPERTS).bitcast(I32)
        S.pairs_i = S.base.take(1).bitcast(I32)
        S.xT = a.take(KD, T)
        branches = a.at
        S.mlaT = a.take(4, T)
        attention = a.at
        S.wuv = a.take(HEADS * VDIM)
        S.ckvT, S.krT = a.take(T), a.take(T)
        S.ckv_rows = a.take(NT, CKV)
        S.qs_c, S.qs_r = a.take(4, 128), a.take(4, 128)
        S.qt_c, S.qt_r = a.take(128), a.take(128)
        S.qslot_c, S.qslot_r = a.take(2, 128), a.take(2, 128)
        queries = a.at
        S.qlat = a.take(HEADS, T)
        S.qrope = a.take(2, T)
        stage_latents(nc, S, I, O)
        stage_prompt_attention(nc, S, I, O)
        a.at = queries
        stage_sample_attention(nc, S, I, O)
        S.recycle()
        a.at = attention
        S.hq = a.take(HGH, T)
        recurrence = a.at
        S.branches = S.big[:, branches:recurrence]
        S.hf = a.take(HGH, T)
        S.hrows = a.take(NT, 1024)
        S.gain_b = a.take(512)
        stage_recurrence_inputs(nc, S, I, O)
        stage_recurrence(nc, S, I, O)
        a.at = recurrence
        S.table = nc.dram_tensor("slot_table", [SLOTS, 2], I32).ap()
        S.x1_dram = nc.dram_tensor("x1_rows", [T + CAP, DM], F32).ap()
        S.y_dram = nc.dram_tensor("y_rows", [T + CAP, DM], F32).ap()
        S.x1 = a.take(NT, DM)
        kept = a.at
        S.merged = a.take(KD, T)
        S.wout = a.take(KD, DM)
        stage_merge(nc, S, I, O)
        stage_route(nc, S, I, O)
        S.recycle()
        a.at = kept
        stage_shared(nc, S, I, O)
        S.repart()
        stage_experts(nc, S, I, O)
        stage_out(nc, S, I, O)


def constants():
    half = ROPE // 2
    pos = np.concatenate([np.arange(TP), PAST + np.arange(TS) % NEW]).astype(np.float32)
    inv = (np.float32(10000.0) ** (-np.arange(half, dtype=np.float32) / np.float32(half))).astype(np.float32)
    ang = (inv[:, None] * pos[None, :]).astype(np.float32)
    cos, sin = np.cos(ang).astype(np.float32), np.sin(ang).astype(np.float32)
    k = np.arange(128)
    causal = np.where(k[None, :] <= k[:, None], 0.0, NEG).astype(np.float32)
    e, t = np.arange(128) // 64, np.arange(128) % NEW
    smask = np.full((128, 4, LAST), NEG, np.float32)
    for p in range(4):
        for r in range(128):
            c = TAIL + NEW * (2 * p + e[r])
            smask[r, p, c:c + t[r] + 1] = 0.0
    tmask = np.where(np.arange(TAIL)[None] <= (k % TAIL)[:, None], 0.0, NEG).astype(np.float32)
    r, c = k[:, None], k[None, :]
    levels = [((r >> l + 1) == (c >> l + 1)) & ((r >> l) % 2 == 0) & ((c >> l) % 2 == 1) for l in range(7)]
    levels = np.stack([np.tile(m, (1, HGH)) for m in levels], 1).astype(np.uint8).reshape(128, -1).view(np.int32)
    rowblock = np.where(np.arange(LAST) < TAIL, 0, 1 + (np.arange(LAST) - TAIL) // NEW)
    blocks = (rowblock[:, None] == np.arange(1 + SAMPLES)[None, :]).astype(np.float32)
    table = np.zeros((SLOTS, 2), np.int32)
    table[:, 0] = T + np.arange(SLOTS) % CAP
    main = np.stack([np.arange(EXPERTS), np.arange(EXPERTS) * VCAP])[None].astype(np.int32)
    token = (128 * np.arange(NT)[None, :] + k[:, None]).astype(np.int32)
    f = np.float32
    return {"c_table": table, "c_main": main, "c_token": token, "c_pid": k[:, None].astype(f),
            "c_before": (k[:, None] < k[None, :]).astype(f), "c_evens": (2 * np.arange(32))[None].astype(f),
            "c_eoff": np.broadcast_to((np.arange(EXPERTS) * VCAP).astype(f), (128, EXPERTS)),
            "c_causal": causal, "c_smask": smask.reshape(128, -1), "c_tmask": tmask,
            "c_levels": levels, "c_blocks": blocks, "c_eye4": np.tile(np.eye(128, dtype=np.float32), (1, HGH)),
            "c_eighth": np.broadcast_to((k % 8)[:, None], (128, 2 * SAMPLES)).astype(np.int32),
            "c_ident": np.eye(128, dtype=np.float32),
            "c_cos": np.tile(np.concatenate([cos, cos]), (4, 1)),
            "c_sin": np.tile(np.concatenate([-sin, sin]), (4, 1))}


OUTS = [(1, SEQ, DM), (SAMPLES, NEW, DM), (1, 1, TP, CKV), (1, 1, TP, ROPE), (1, 1, HGH, HGD, HGD),
        (1, SAMPLES, NEW, CKV), (1, SAMPLES, NEW, ROPE), (1, SAMPLES, HGH, HGD, HGD)]


def kernel(**inputs):
    import concourse.bacc as bacc
    from concourse.bass_utils import run_bass_kernel_spmd as run

    nc = bacc.Bacc("TRN2", target_bir_lowering=False, num_devices=1)
    arrays, I = {}, {}
    pt = inputs["page_table"]
    for name in ("ln1_g", "ln1_b", "ln2_g", "ln2_b", "router_bias"):
        inputs[name] = np.broadcast_to(inputs[name], (128, inputs[name].shape[1]))
    inputs = dict(inputs, hg_norm=np.tile(np.broadcast_to(inputs["hg_norm"], (128, HGD)), (1, HGH)), page_table=np.broadcast_to(pt.reshape(2 * SAMPLES, 16).T[:, None, :], (16, 8, 2 * SAMPLES)).reshape(128, -1))
    for name, a in {**inputs, **constants()}.items():
        a = np.ascontiguousarray(a)
        arrays[f"in_{name}"] = a
        I[name] = nc.dram_tensor(f"in_{name}", a.shape, mybir.dt.from_np(a.dtype), kind="ExternalInput").ap()
    O = [nc.dram_tensor(f"out_{i}", s, F32, kind="ExternalOutput").ap() for i, s in enumerate(OUTS)]
    build(nc, I, O)
    r = run(nc, [arrays], core_ids=[0])
    return tuple(r.results[0][f"out_{i}"] for i in range(len(OUTS)))
```
